# Optimizing a Trainium2 kernel written in Bass

```python
import jax, jax.numpy as jnp
from jax import lax
import numpy as np

D_MODEL = 1024
BATCH = 1
SEQ = 1024
DEPTH = 2
DEC_BATCH = 8
DEC_SEQ = 1
PAST_LEN = 1024
PAGE_SIZE = 128

N_MIXERS = 2
N_CONV_LAYERS = (DEPTH + 1) // 2
N_ATTN_LAYERS = DEPTH // 2
CONV_WIDTH = 31
N_HEADS = 16
N_KV_HEADS = 4
HEAD_DIM = D_MODEL // N_HEADS
GROUP = N_HEADS // N_KV_HEADS
ROT_DIM = HEAD_DIM // 4
ROPE_THETA = 500000.0
WINDOW = 128
BLOCK = 128
D_FF = 11 * D_MODEL // 4
FFN_CONV_WIDTH = 3
EPS = 1e-6

kernel_name = "hybrid_conformer_conv_swa_sink_convffn_step"

def _rmsnorm(x, g):
    xf = x.astype(jnp.float32)
    y = xf * lax.rsqrt(jnp.mean(xf * xf, axis=-1, keepdims=True) + EPS)
    return (y * g.astype(jnp.float32)).astype(x.dtype)

def _layernorm(x, g, b):
    xf = x.astype(jnp.float32)
    mu = jnp.mean(xf, axis=-1, keepdims=True)
    var = jnp.mean(jnp.square(xf - mu), axis=-1, keepdims=True)
    y = (xf - mu) * lax.rsqrt(var + EPS)
    return (y * g.astype(jnp.float32) + b.astype(jnp.float32)).astype(x.dtype)

def _causal_dwconv(x_hist, w, b):
    y = lax.conv_general_dilated(
        x_hist, w[:, None, :].astype(x_hist.dtype), window_strides=(1,), padding='VALID',
        dimension_numbers=('NWC', 'WIO', 'NWC'), feature_group_count=w.shape[-1])
    return y + b

def _rope(x, pos):
    inv = 1.0 / (ROPE_THETA ** (jnp.arange(0, ROT_DIM, 2, dtype=jnp.float32) / ROT_DIM))
    ang = pos.astype(jnp.float32)[:, None] * inv[None, :]
    cos = jnp.cos(ang)[:, None, :]
    sin = jnp.sin(ang)[:, None, :]
    half = ROT_DIM // 2
    xr = x[..., :ROT_DIM].astype(jnp.float32)
    x1, x2 = xr[..., :half], xr[..., half:]
    rot = jnp.concatenate([x1 * cos - x2 * sin, x2 * cos + x1 * sin], axis=-1)
    return jnp.concatenate([rot.astype(x.dtype), x[..., ROT_DIM:]], axis=-1)

def _sink_attention(q, k, v, q_pos, k_pos, sinks):
    s = jnp.einsum('bnqkgd,bnskd->bnkgqs', q, k).astype(jnp.float32) * (HEAD_DIM ** -0.5)
    diff = q_pos[:, :, None] - k_pos[:, None, :]
    mask = (diff >= 0) & (diff <= WINDOW) & (k_pos[:, None, :] >= 0)
    s = jnp.where(mask[None, :, None, None, :, :], s, -jnp.inf)
    sink = sinks.astype(jnp.float32).reshape(N_KV_HEADS, GROUP)[None, None, :, :, None, None]
    m = jnp.maximum(jnp.max(s, axis=-1, keepdims=True), sink)
    p = jnp.exp(s - m)
    p = p / (jnp.sum(p, axis=-1, keepdims=True) + jnp.exp(sink - m))
    return jnp.einsum('bnkgqs,bnskd->bnqkgd', p.astype(v.dtype), v)

def _swa_mixer(h, start, k_buf, v_buf, w_qkv, sinks, w_o):
    n, t, _ = h.shape
    qkv = h @ w_qkv
    q = qkv[..., :N_HEADS * HEAD_DIM].reshape(n, t, N_HEADS, HEAD_DIM)
    k = qkv[..., N_HEADS * HEAD_DIM:(N_HEADS + N_KV_HEADS) * HEAD_DIM].reshape(n, t, N_KV_HEADS, HEAD_DIM)
    v = qkv[..., (N_HEADS + N_KV_HEADS) * HEAD_DIM:].reshape(n, t, N_KV_HEADS, HEAD_DIM)
    pos = start + jnp.arange(t)
    q = _rope(q, pos)
    k = _rope(k, pos)
    if k_buf is None:
        nb = t // BLOCK
        qb = q.reshape(n, nb, BLOCK, N_KV_HEADS, GROUP, HEAD_DIM)
        pad = jnp.zeros((n, BLOCK, N_KV_HEADS, HEAD_DIM), k.dtype)
        kb = jnp.concatenate([pad, k], axis=1).reshape(n, nb + 1, BLOCK, N_KV_HEADS, HEAD_DIM)
        vb = jnp.concatenate([pad, v], axis=1).reshape(n, nb + 1, BLOCK, N_KV_HEADS, HEAD_DIM)
        kb = jnp.concatenate([kb[:, :-1], kb[:, 1:]], axis=2)
        vb = jnp.concatenate([vb[:, :-1], vb[:, 1:]], axis=2)
        blk = jnp.arange(nb)[:, None]
        q_pos = blk * BLOCK + jnp.arange(BLOCK)[None, :]
        k_pos = (blk - 1) * BLOCK + jnp.arange(2 * BLOCK)[None, :]
        o = _sink_attention(qb, kb, vb, q_pos, k_pos, sinks)
        new_k, new_v = k[:, t - WINDOW:], v[:, t - WINDOW:]
    else:
        buf = k_buf.shape[1]
        k_all = jnp.concatenate([k_buf, k], axis=1)
        v_all = jnp.concatenate([v_buf, v], axis=1)
        qb = q.reshape(n, 1, t, N_KV_HEADS, GROUP, HEAD_DIM)
        q_pos = (start + jnp.arange(t))[None, :]
        k_pos = (start - buf + jnp.arange(buf + t))[None, :]
        o = _sink_attention(qb, k_all[:, None], v_all[:, None], q_pos, k_pos, sinks)
        new_k, new_v = k_all[:, -buf:], v_all[:, -buf:]
    out = o.reshape(n, t, N_HEADS * HEAD_DIM) @ w_o
    return out, new_k, new_v

def _conv_module(h, hist, w_pw1, b_pw1, w_dw, b_dw, ln_g, ln_b, w_pw2, b_pw2):
    a = h @ w_pw1 + b_pw1
    glu = a[..., :D_MODEL] * jax.nn.sigmoid(a[..., D_MODEL:])
    if hist is None:
        hist = jnp.zeros((h.shape[0], CONV_WIDTH - 1, D_MODEL), glu.dtype)
    full = jnp.concatenate([hist, glu], axis=1)
    c = jax.nn.silu(_layernorm(_causal_dwconv(full, w_dw, b_dw), ln_g, ln_b))
    return c @ w_pw2 + b_pw2, full[:, -(CONV_WIDTH - 1):]

def _conv_ffn(h, hist, w_in, w_dw, b_dw, w_down):
    gu = h @ w_in
    g, u = gu[..., :D_FF], gu[..., D_FF:]
    if hist is None:
        hist = jnp.zeros((h.shape[0], FFN_CONV_WIDTH - 1, D_FF), g.dtype)
    full = jnp.concatenate([hist, g], axis=1)
    gc = _causal_dwconv(full, w_dw, b_dw)
    return (jax.nn.silu(gc) * u) @ w_down, full[:, -(FFN_CONV_WIDTH - 1):]

def _trunk(x, start, st_conv, st_k, st_v, st_ffn, norm_mix, norm_ffn, norm_final,
           conv_w_pw1, conv_b_pw1, conv_w_dw, conv_b_dw, conv_ln_g, conv_ln_b, conv_w_pw2, conv_b_pw2,
           attn_w_qkv, attn_sinks, attn_w_o, ffn_w_in, ffn_w_dw, ffn_b_dw, ffn_w_down):
    new_conv, new_k, new_v, new_ffn = [], [], [], []
    for i in range(DEPTH):
        j = i // N_MIXERS
        h = _rmsnorm(x, norm_mix[i])
        if i % N_MIXERS == 0:
            hist = None if st_conv is None else st_conv[j]
            out, nh = _conv_module(h, hist, conv_w_pw1[j], conv_b_pw1[j], conv_w_dw[j], conv_b_dw[j],
                                   conv_ln_g[j], conv_ln_b[j], conv_w_pw2[j], conv_b_pw2[j])
            new_conv.append(nh)
        else:
            kb = None if st_k is None else st_k[j]
            vb = None if st_v is None else st_v[j]
            out, nk, nv = _swa_mixer(h, start, kb, vb, attn_w_qkv[j], attn_sinks[j], attn_w_o[j])
            new_k.append(nk)
            new_v.append(nv)
        x = x + out
        h = _rmsnorm(x, norm_ffn[i])
        hist = None if st_ffn is None else st_ffn[i]
        out, nh = _conv_ffn(h, hist, ffn_w_in[i], ffn_w_dw[i], ffn_b_dw[i], ffn_w_down[i])
        new_ffn.append(nh)
        x = x + out
    y = _rmsnorm(x, norm_final)
    return y, jnp.stack(new_conv), jnp.stack(new_k), jnp.stack(new_v), jnp.stack(new_ffn)

def setup_inputs(seed: int = 0) -> dict:
    key = jax.random.key(seed)
    ks = jax.random.split(key, 26)

    def nrm(k, shape, scale=1.0):
        return jax.random.normal(k, shape, jnp.float32) * scale

    buf = min(WINDOW, PAST_LEN)
    qkv_w = (N_HEADS + 2 * N_KV_HEADS) * HEAD_DIM
    return {
        "x_prompt": nrm(ks[0], (BATCH, SEQ, D_MODEL)),
        "x_sample": nrm(ks[1], (DEC_BATCH, DEC_SEQ, D_MODEL)),
        "state_conv": nrm(ks[2], (N_CONV_LAYERS, DEC_BATCH, CONV_WIDTH - 1, D_MODEL), 0.5),
        "cache_k": nrm(ks[3], (N_ATTN_LAYERS, DEC_BATCH, buf, N_KV_HEADS, HEAD_DIM)),
        "cache_v": nrm(ks[4], (N_ATTN_LAYERS, DEC_BATCH, buf, N_KV_HEADS, HEAD_DIM)),
        "state_ffn": nrm(ks[5], (DEPTH, DEC_BATCH, FFN_CONV_WIDTH - 1, D_FF)),
        "norm_mix": 1.0 + nrm(ks[6], (DEPTH, D_MODEL), 0.01),
        "norm_ffn": 1.0 + nrm(ks[7], (DEPTH, D_MODEL), 0.01),
        "norm_final": 1.0 + nrm(ks[8], (D_MODEL,), 0.01),
        "conv_w_pw1": nrm(ks[9], (N_CONV_LAYERS, D_MODEL, 2 * D_MODEL), D_MODEL ** -0.5),
        "conv_b_pw1": nrm(ks[10], (N_CONV_LAYERS, 2 * D_MODEL), 0.01),
        "conv_w_dw": nrm(ks[11], (N_CONV_LAYERS, CONV_WIDTH, D_MODEL), CONV_WIDTH ** -0.5),
        "conv_b_dw": nrm(ks[12], (N_CONV_LAYERS, D_MODEL), 0.01),
        "conv_ln_g": 1.0 + nrm(ks[13], (N_CONV_LAYERS, D_MODEL), 0.01),
        "conv_ln_b": nrm(ks[14], (N_CONV_LAYERS, D_MODEL), 0.01),
        "conv_w_pw2": nrm(ks[15], (N_CONV_LAYERS, D_MODEL, D_MODEL), D_MODEL ** -0.5),
        "conv_b_pw2": nrm(ks[16], (N_CONV_LAYERS, D_MODEL), 0.01),
        "attn_w_qkv": nrm(ks[17], (N_ATTN_LAYERS, D_MODEL, qkv_w), D_MODEL ** -0.5),
        "attn_sinks": nrm(ks[18], (N_ATTN_LAYERS, N_HEADS), 0.5),
        "attn_w_o": nrm(ks[19], (N_ATTN_LAYERS, N_HEADS * HEAD_DIM, D_MODEL), (N_HEADS * HEAD_DIM) ** -0.5),
        "ffn_w_in": nrm(ks[20], (DEPTH, D_MODEL, 2 * D_FF), D_MODEL ** -0.5),
        "ffn_w_dw": nrm(ks[21], (DEPTH, FFN_CONV_WIDTH, D_FF), FFN_CONV_WIDTH ** -0.5),
        "ffn_b_dw": nrm(ks[22], (DEPTH, D_FF), 0.01),
        "ffn_w_down": nrm(ks[23], (DEPTH, D_FF, D_MODEL), D_FF ** -0.5),
    }

def reference(x_prompt, x_sample, state_conv, cache_k, cache_v, state_ffn, norm_mix, norm_ffn, norm_final,
              conv_w_pw1, conv_b_pw1, conv_w_dw, conv_b_dw, conv_ln_g, conv_ln_b, conv_w_pw2, conv_b_pw2,
              attn_w_qkv, attn_sinks, attn_w_o, ffn_w_in, ffn_w_dw, ffn_b_dw, ffn_w_down):
    y_prompt, conv_p, k_p, v_p, ffn_p = _trunk(
        x_prompt, 0, None, None, None, None, norm_mix, norm_ffn, norm_final,
        conv_w_pw1, conv_b_pw1, conv_w_dw, conv_b_dw, conv_ln_g, conv_ln_b, conv_w_pw2, conv_b_pw2,
        attn_w_qkv, attn_sinks, attn_w_o, ffn_w_in, ffn_w_dw, ffn_b_dw, ffn_w_down)
    y_sample, conv_s, k_s, v_s, ffn_s = _trunk(
        x_sample, PAST_LEN, state_conv, cache_k, cache_v, state_ffn, norm_mix, norm_ffn, norm_final,
        conv_w_pw1, conv_b_pw1, conv_w_dw, conv_b_dw, conv_ln_g, conv_ln_b, conv_w_pw2, conv_b_pw2,
        attn_w_qkv, attn_sinks, attn_w_o, ffn_w_in, ffn_w_dw, ffn_b_dw, ffn_w_down)
    return (y_prompt, y_sample, conv_p, conv_s, k_p, v_p, k_s, v_s, ffn_p, ffn_s)


_drawn_inputs = setup_inputs


def setup_inputs(seed=0):
    import zlib

    import numpy as np

    out = dict(_drawn_inputs(seed))
    spreads = {}
    factors = {'norm_mix': 4.711,
     'norm_ffn': 5.08,
     'norm_final': 34.863,
     'conv_b_pw1': 5.357,
     'conv_b_dw': 4.128,
     'conv_ln_g': 7.02,
     'conv_ln_b': 8.0,
     'conv_b_pw2': 4.699,
     'attn_sinks': 64.0,
     'ffn_b_dw': 8.0}
    for name, (base, spread) in spreads.items():
        noise = np.random.default_rng([zlib.crc32(name.encode()), seed]).standard_normal(out[name].shape)
        drawn = base * np.exp(spread * noise) if base else spread * noise
        out[name] = __import__('jax').numpy.asarray(drawn.astype(out[name].dtype))
    for name, factor in factors.items():
        out[name] = (out[name] * factor).astype(out[name].dtype)
    return out
```

```python
from contextlib import ExitStack, contextmanager

import numpy as np

import concourse.bass as bass
from concourse import mybir

F32 = mybir.dt.float32
F32R = mybir.dt.float32r
ALU = mybir.AluOpType
ACT = mybir.ActivationFunctionType
AX = mybir.AxisListType.X

P = 128
D = 1024
KT = D // P
SEQ = 1024
NS = 8
T = SEQ + NS
NCH = 3
CH = T // NCH
BANK = 512
NB = SEQ // P
F = 2816
FT = F // P
CW = 31
HIST = CW - 1
NT = 10
NTA = 7
K_TILE = (6, 0)
HD = 64
GROUP = 4
NH = 16
NKV = 4
ROT = HD // 4
WIN = 128
EPS = 1e-6
SCALE = HD ** -0.5
MASKED = -1e30
PADK = P + T
WKC = HIST + T
WKP = -(-WKC // 8) * 8

R_MIX, R_FFN, R_FIN, R_B1, R_DW, R_BDW, R_LNG, R_LNB, R_B2 = 0, 2, 4, 5, 7, 38, 39, 40, 41
NPAR = 42
FR_W, FR_B, FR_ST, NFR = 0, 3, 4, 20

C_ID, C_ONE, C_PERM, C_SEL = 0, 128, 256, 384
NCONST = 392


def constants():
    ident = np.eye(P, dtype=np.float32)
    perm = np.zeros((P, P), np.float32)
    cos = np.ones((P, T), np.float32)
    sin = np.zeros((P, T), np.float32)
    half = ROT // 2
    theta = np.float32(500000.0)
    inv = (np.float32(1.0) / (theta ** (np.arange(0, ROT, 2, dtype=np.float32) / np.float32(ROT)))).astype(np.float32)
    pos = np.concatenate([np.arange(SEQ), np.full(NS, SEQ)]).astype(np.float32)
    ang = (inv[:, None] * pos[None, :]).astype(np.float32)
    for r in range(P):
        d = r % HD
        if d < ROT:
            perm[r - d + (d + half) % ROT, r] = 1.0
            cos[r] = np.cos(ang[d % half])
            sin[r] = np.sin(ang[d % half]) * np.float32(-1.0 if d < half else 1.0)
    sel = (np.arange(P)[:, None] // (P // NS) == np.arange(NS)[None, :]).astype(np.float32)
    small = np.concatenate([ident, np.ones((P, P), np.float32), perm, sel], axis=1)
    q, s = np.arange(P)[:, None], np.arange(2 * P)[None, :]
    band = (s >= q) & (s <= q + WIN)
    rest = np.where(band, np.float32(0), np.float32(MASKED))
    first = np.where(band & (s >= P), np.float32(0), np.float32(MASKED))
    mask = np.concatenate([first, first, rest, rest], axis=1).astype(np.float32)
    return small, mask, np.concatenate([cos, sin], axis=1)


class Count:

    def __init__(self):
        self.n, self.turn = 0, 0

    def up(self):
        self.n += 1
        return 1

    def next(self, by=1):
        self.n += by
        return self.at()

    def at(self, back=0):
        assert self.n - back > 0, "no wait is for less than one signal"
        return self.turn + (self.n - back)

    def due(self, back=0):
        return self.n - back > 0


@contextmanager
def turns(eng, first, last, counts):
    start = {c: c.n for c in counts}
    with eng.Fori(first, last) as i:
        for c, per in counts.items():
            c.turn = (i - first) * per if first else i * per
        yield i
        for c, per in counts.items():
            assert c.n - start[c] == per, (c.n - start[c], per)
    for c, per in counts.items():
        c.turn, c.n = 0, start[c] + per * (last - first)


def build(nc, a):
    ctx = ExitStack()
    with ctx:
        def sb(name, shape, dt=F32, stack=ctx):
            return stack.enter_context(nc.sbuf_tensor(name, shape, dt))

        def sem(name):
            return ctx.enter_context(nc.semaphore(name))

        X = sb("X", [P, KT, T])
        W = sb("W", [P, 2, 2, D], F32R)
        RAW = sb("RAW", [P, 2, D])
        CST = sb("CST", [P, NCONST])
        PAR = sb("PAR", [P, KT, NPAR])
        FPAR = sb("FPAR", [P, FT, 2 * NFR])
        TOK = sb("TOK", [P, 4, NB + 1])
        CKEEP = sb("CKEEP", [P, KT, HIST + NS])
        NSINK = sb("NSINK", [P, NH])
        SINKC = sb("SINKC", [NH, 2])
        SMALL = sb("SMALL", [P, 2, 6, GROUP])
        with ExitStack() as s:
            sb("skip_tiles_0_1", [P, 2, WKP], F32, s)
            GSPLIT = sb("GSPLIT", [P, 2, WKP], F32R, s)
            sb("skip_tile_4", [P, WKP], F32, s)
            DIAGB = sb("DIAGB", [P, 2, NT - NTA, P], F32R, s)
            sb("skip_tiles_6_8", [P, 4 * WKP - 2 * (NT - NTA) * P], F32, s)
            DIAGA = sb("DIAGA", [P, 2, NTA, P], F32R, s)
        WK = sb("WK", [P, 9, WKP])
        GKEEP = sb("GKEEP", [P, 2, FT, 2 + NS])
        PBLK = sb("PBLK", [P, NS, NS, NH])
        TAPLO = WK[:, 6, 256:256 + KT * NT].rearrange("p (m k) -> p m k", m=KT)
        TAPHI = GSPLIT[:, 0, 0:KT * NT].rearrange("p (m k) -> p m k", m=KT)
        sb("diagonals_end", [P, max(0, 2 * NTA * P - 2 * FT * (2 + NS) - NS * NS * NH)])
        with ExitStack() as s:
            XIN = sb("XIN", [P, NB, D], F32, s)
        with ExitStack() as s:
            CONV = sb("CONV", [P, KT, T], F32, s)
        with ExitStack() as s:
            MID = sb("MID", [P, 2, 2, T], F32R, s)
        with ExitStack() as s:
            YOUT = sb("YOUT", [P, NB, D], F32, s)
        QA = sb("QA", [P, 2, GROUP, T])
        with ExitStack() as s:
            H = sb("H", [P, 2, KT, T], F32R, s)
        KR = sb("KR", [P, 2, 2, PADK], F32R)
        VR = sb("VR", [P, 2, NB + 1, NKV * HD], F32R)
        MASK = sb("MASK", [P, 2, BANK], F32R)
        QS = sb("QS", [P, 2, 2, BANK], F32R)
        PX = sb("PX", [P, 2, GROUP, 2 * P])
        PT = sb("PT", [P, 2, 2, BANK], F32R)
        IDR = sb("IDR", [P, P], F32R)
        PS = ctx.enter_context(nc.psum_tensor("PS", [P, 8, BANK], F32))

        IDENT, ONES, PERM = (CST[:, c:c + P] for c in (C_ID, C_ONE, C_PERM))
        SEL = CST[:, C_SEL:C_SEL + NS]
        RS, ACC = WK[:, 0, 0:T], WK[:, 1, 0:T]
        SQ = [WK[:, 2, 0:T], WK[:, 3, 0:T]]
        DG = WK[:, 6, 0:T]
        COS, SIN = WK[:, 7, 0:T], WK[:, 8, 0:T]

        def chunks(ap):
            return ap.rearrange("p (c n) -> p c n", c=NCH)

        def par(m, r):
            if isinstance(m, int):
                return PAR[:, m, r:r + 1]
            return PAR[:, bass.ds(m, 1), r:r + 1].rearrange("p a b -> p (a b)")

        def fpar(f, r, n=1):
            if isinstance(f, int):
                return FPAR[:, f, r:r + n]
            return FPAR[:, bass.ds(f, 1), r:r + n].rearrange("p a b -> p (a b)")

        def tile(t, m, lo=0, hi=T):
            if isinstance(m, int):
                return t[:, m, lo:hi]
            return t[:, bass.ds(m, 1), lo:hi].rearrange("p a b -> p (a b)")

        def htile(part, m):
            if isinstance(m, int):
                return H[:, part, m, :]
            return H[:, part, bass.ds(m, 1), :].rearrange("p a b -> p (a b)")

        s_const = sem("const_loaded")
        s_rows = sem("rows_loaded")
        s_x = sem("x_loaded")
        s_tab = sem("tables_loaded")
        s_cache = sem("cache_loaded")
        s_raw = [sem("raw_loaded0"), sem("raw_loaded1")]
        s_hi = sem("weight_hi")
        s_go = sem("split_may_start")
        s_w = sem("weight_ready")
        s_wstart = sem("weight_started")
        s_tr = sem("transposed")
        s_trr = sem("transpose_taken")
        s_mm = sem("dense_done")
        s_pr = sem("dense_taken")
        s_sq = sem("square_ready")
        s_acc = sem("accumulated")
        s_hh = sem("h_hi_ready")
        s_h = sem("h_ready")
        s_tok = sem("token_sums")
        s_tokd = sem("token_scalars_dve")
        s_toka = sem("token_scalars_act")
        s_dg = sem("diagonal_ready")
        s_bc = sem("broadcast_done")
        s_bcr = sem("broadcast_taken")
        s_v = sem("dve_own")
        s_a = sem("act_own")
        s_gate = sem("gate_scaled")
        s_sig = sem("sigmoid_ready")
        s_glu = sem("glu_ready")
        s_tap0 = sem("first_tap")
        s_taplo = sem("tap_weights_lo")
        s_taphi = sem("tap_weights_hi")
        s_gh = sem("glu_hi")
        s_gs = sem("glu_split")
        s_diag = sem("tap_diagonals_ready")
        s_td = sem("last_taps_done")
        s_tt = sem("last_taps_taken")
        s_conv = sem("conv_done")
        s_g = sem("gate_rows")
        s_t2 = sem("last_tap")
        s_gc = sem("gate_conv")
        s_silu = sem("silu_ready")
        s_m = sem("mid_ready")
        s_mh = sem("mid_hi")
        s_mid = sem("mid_split")
        s_heads = sem("heads_ready")
        s_kvh = sem("kv_hi")
        s_kv = sem("kv_ready")
        s_kvo = sem("kv_turned")
        s_kvr = sem("kv_rows_taken")
        s_qh = sem("q_hi")
        s_qs = sem("q_split")
        s_sc = sem("scores_done")
        s_nm = sem("negative_max")
        s_ex = sem("exp_done")
        s_pn = sem("probs_ready")
        s_pt = sem("probs_turned")
        s_pth = sem("probs_hi")
        s_ptl = sem("probs_split")
        s_pv = sem("heads_done")
        s_ov = sem("heads_taken")
        s_small = sem("small_values")
        s_svx = sem("sample_scores_shifted")
        s_sm = sem("sample_mm")
        s_sv = sem("sample_dve")
        s_sa = sem("sample_act")
        s_xg = sem("x_gained")
        s_st = sem("stores")

        up = "(k p) n -> p k n"
        w_pw1 = a["conv_w_pw1"][0].rearrange(up, p=P)
        w_pw2 = a["conv_w_pw2"][0].rearrange(up, p=P)
        w_qkv = a["attn_w_qkv"][0].rearrange(up, p=P)
        w_in = [a["ffn_w_in"][l].rearrange(up, p=P) for l in range(2)]
        w_dn = [a["ffn_w_down"][l].rearrange("(t p) n -> p t n", p=P) for l in range(2)]
        w_o = a["attn_w_o"][0].rearrange("(a h g d) n -> h d a g n", a=2, h=2, g=GROUP)

        acc_marks = []
        GROWS = [WK[:, 6:9, :].rearrange("p a n -> p (a n)"), WK[:, 0:3, :].rearrange("p a n -> p (a n)")]
        LNSQ = [WK[:, 2, 0:T], WK[:, 5, 0:T]]
        UNITS = [(n, p, hf) for n in range(NB) for p in range(2) for hf in range(2)]
        HEADS, KV_READY = 2 + 2 * KT, 5
        ROW_DMAS = 20
        STORES = 23
        block = ctx.enter_context(nc.Block())

        @block.sync
        def _(sp):
            ready = Count()
            n = [0]

            def load(src_halves, slot):
                if n[0] >= 2:
                    sp.wait_ge(s_w, ready.at(1))
                n[0] += 1
                for h, src in enumerate(src_halves):
                    dst = RAW[h * HD:(h + 1) * HD, slot, :]
                    dst = dst.rearrange("p (k n) -> p k n", k=src.shape[-2])
                    sp.dma_start(dst, src).then_inc(s_raw[slot], 16)
                ready.n += 1

            def halves(w, col):
                return [w[h * HD:(h + 1) * HD, :, bass.ds(col, P)] for h in range(2)]

            def down(l, i, half):
                return [w_dn[l][h * HD:(h + 1) * HD, bass.ds(i * 2, 2), half * BANK:(half + 1) * BANK]
                        for h in range(2)]

            def ffn(l):
                def gate(f, slot):
                    load(halves(w_in[l], f * P), slot)

                def upp(f, slot):
                    load(halves(w_in[l], f * P + F), slot)
                gate(0, 0)
                upp(0, 1)
                gate(1, 0)
                upp(1, 1)
                with turns(sp, 1, FT // 2, {ready: 6}) as i:
                    gate(i * 2, 0)
                    load(down(l, i - 1, 0), 1)
                    load(down(l, i - 1, 1), 0)
                    upp(i * 2, 1)
                    gate(i * 2 + 1, 0)
                    upp(i * 2 + 1, 1)
                load(down(l, FT // 2 - 1, 0), 0)
                load(down(l, FT // 2 - 1, 1), 1)

            load(halves(w_pw1, 0), 0)
            load(halves(w_pw1, D), 1)
            with turns(sp, 1, KT, {ready: 2}) as i:
                load(halves(w_pw1, i * P), 0)
                load(halves(w_pw1, i * P + D), 1)
            with turns(sp, 0, KT // 2, {ready: 2}) as i:
                load(halves(w_pw2, i * 2 * P), 0)
                load(halves(w_pw2, i * 2 * P + P), 1)
            ffn(0)
            vcol, kcol = (NH + NKV) * HD, NH * HD
            for j, col in enumerate([vcol, vcol + P, kcol, kcol + P]):
                load(halves(w_qkv, col), j % 2)
            with turns(sp, 0, KT // 2, {ready: 2}) as i:
                load(halves(w_qkv, i * 2 * P), 0)
                load(halves(w_qkv, i * 2 * P + P), 1)

            def wo(m, slot):
                sp.wait_ge(s_w, ready.at(1))
                for h in range(2):
                    for b in range(2):
                        dst = RAW[h * HD:(h + 1) * HD, slot, b * BANK:(b + 1) * BANK]
                        sp.dma_start(dst.rearrange("p (g n) -> p g n", g=GROUP),
                                     w_o[h, :, b, :, bass.ds(m * P, P)]).then_inc(s_raw[slot], 8 * 2)
                ready.n += 1
            with turns(sp, 0, KT // 2, {ready: 2}) as i:
                wo(i * 2, 0)
                wo(i * 2 + 1, 1)
            ffn(1)
            yr = Count()
            yr.n = 2 + KT + 5
            for n_ in range(NB):
                sp.wait_ge(s_trr, yr.next())
                sp.dma_start(a["y_prompt"][0, n_ * P:(n_ + 1) * P, :], YOUT[:, n_, :]).then_inc(s_st, 16)
            sp.wait_ge(s_trr, yr.next())
            sp.dma_start(a["y_sample"][:, 0, :], WK[0:NS, 4, 0:D]).then_inc(s_st, 16)
            sp.wait_ge(s_st, 16 * STORES)

        @block.gpsimd
        def _(pool):
            started, ready, hi = Count(), Count(), Count()
            raw = [Count(), Count()]

            def split(slot, per, free):
                pool.wait_ge(s_raw[slot], raw[slot].next(per))
                if free:
                    pool.wait_ge(s_wstart, started.at())
                started.n += 1
                pool.sem_inc(s_go, 1)
                nc.gpsimd.tensor_copy(W[:, slot, 0, :], RAW[:, slot, :]).then_inc(s_hi, hi.up())
                pool.wait_ge(s_hi, hi.at())
                nc.gpsimd.tensor_tensor(W[:, slot, 1, :], RAW[:, slot, :],
                                                  W[:, slot, 0, :].bitcast(F32), ALU.subtract).then_inc(s_w, ready.up())

            def stretch(count, per=32):
                with turns(pool, 0, count // 2, {started: 2, ready: 2, hi: 2, raw[0]: per, raw[1]: per}):
                    split(0, per, True)
                    split(1, per, True)

            split(0, 32, False)
            split(1, 32, True)
            n_ffn = 3 * FT
            stretch(2 * KT - 2 + KT + n_ffn + 4 + KT)
            stretch(KT, 64)
            stretch(n_ffn)

        def attention_dve(dve):
            v = nc.vector
            own = Count()
            kvh, qh, qs = Count(), Count(), Count()
            sc, nm, ex, pn = Count(), Count(), Count(), Count()
            pth, ptl = Count(), Count()
            sv = Count()
            small = Count()

            v.memset(KR[:, :, :, 0:P].bitcast(F32), 0.0).then_inc(s_kv, own.up())
            v.memset(VR[:, :, 0, :].bitcast(F32), 0.0).then_inc(s_kv, own.up())
            for p in range(2):
                dve.wait_ge(s_kvh, kvh.next())
                v.tensor_tensor(KR[:, 1, p, P:PADK], WK[:, K_TILE[p], 0:T], KR[:, 0, p, P:PADK].bitcast(F32),
                                        ALU.subtract).then_inc(s_kv, own.up())
            dve.wait_ge(s_kvo, 1)
            v.tensor_copy(WK[0:NS, 8, 0:BANK], PS[0:NS, 4, :])
            v.tensor_copy(WK[:, 8, BANK:BANK + 256], PS[:, 5, 0:256])
            v.tensor_copy(WK[:, 8, BANK + 256:2 * BANK], PS[:, 3, 256:BANK]).then_inc(s_kvr, 1)
            dve.wait_ge(s_kvh, kvh.next(3))
            v.tensor_tensor(VR[:, 1, 1:NB + 1, :].rearrange("p (a b) n -> p a (b n)", b=2), PS[:, 0:4, :],
                                    VR[:, 0, 1:NB + 1, :].rearrange("p (a b) n -> p a (b n)", b=2).bitcast(F32),
                                    ALU.subtract).then_inc(s_kv, own.up())
            assert own.n == KV_READY

            def q_lo(n, p):
                dve.wait_ge(s_qh, qh.next())
                v.tensor_tensor(QS[:, p, 1, :].rearrange("p (g n) -> p g n", g=GROUP),
                                       QA[:, p, :, n * P:(n + 1) * P],
                                       QS[:, p, 0, :].rearrange("p (g n) -> p g n", g=GROUP).bitcast(F32), ALU.subtract).then_inc(s_qs, qs.up())

            def stats(n, p, hf):
                j = 2 * p + hf
                dve.wait_ge(s_sc, sc.next())
                v.tensor_reduce(SMALL[:, hf, 0, :],
                                            PS[:, 2 * hf:2 * hf + 2, :].rearrange("p a (g n) -> p (a g) n", g=2), AX, ALU.max).then_inc(s_small, small.up())
                dve.wait_ge(s_small, small.at())
                nsink = NSINK[:, j * GROUP:(j + 1) * GROUP]
                v.scalar_tensor_tensor(SMALL[:, hf, 1, :], SMALL[:, hf, 0, :], -SCALE, nsink, ALU.mult, ALU.min).then_inc(s_nm, nm.up())
                dve.wait_ge(s_nm, nm.at())
                v.tensor_tensor(SMALL[:, hf, 2, :], SMALL[:, hf, 1, :], nsink, ALU.subtract).then_inc(s_nm, nm.up())

            def norm(n, p, hf):
                dve.wait_ge(s_ex, ex.next())
                v.tensor_tensor(SMALL[:, hf, 5, :], SMALL[:, hf, 3, :], SMALL[:, hf, 4, :], ALU.add).then_inc(s_small, small.up())
                dve.wait_ge(s_small, small.at())
                v.reciprocal(SMALL[:, hf, 0, :], SMALL[:, hf, 5, :]).then_inc(s_small, small.up())
                dve.wait_ge(s_small, small.at())
                v.tensor_tensor(PX[:, hf], PX[:, hf],
                                       SMALL[:, hf, 0, :].unsqueeze(2).broadcast_to((P, GROUP, 2 * P)), ALU.mult).then_inc(s_pn, pn.up())

            def probs_lo():
                dve.wait_ge(s_pth, pth.next())
                v.tensor_tensor(PT[:, 1], PS[:, 4:6, :], PT[:, 0].bitcast(F32), ALU.subtract).then_inc(s_ptl, ptl.up())

            q_lo(0, 0)
            stats(*UNITS[0])
            norm(*UNITS[0])
            for u in range(len(UNITS)):
                if u + 2 < len(UNITS) and UNITS[u + 2][2] == 0:
                    q_lo(*UNITS[u + 2][:2])
                if u + 1 < len(UNITS):
                    stats(*UNITS[u + 1])
                probs_lo()
                if u + 1 < len(UNITS):
                    norm(*UNITS[u + 1])

            smm, sa = Count(), Count()
            Z = WK[:, 6, :]
            qb = Z[:, 0:256].rearrange("p (a b h) -> p a b h", a=2, b=NS)
            dve.wait_ge(s_sm, smm.next())
            v.tensor_copy(WK[:, 4:6, 0:D], PS[:, 0:4, :].rearrange("p (a b) n -> p a (b n)", b=2)).then_inc(s_sv, sv.up())
            v.memset(Z[:, 0:256], 0.0).then_inc(s_small, small.up())
            dve.wait_ge(s_small, small.at())
            for p in range(2):
                for hf in range(2):
                    rows, h0 = slice(hf * HD, (hf + 1) * HD), (2 * p + hf) * GROUP
                    last = v.tensor_copy(qb[rows, p, :, h0:h0 + GROUP].rearrange("p b g -> p g b"), QA[rows, p, :, SEQ:T])
            last.then_inc(s_sv, sv.up())
            dve.wait_ge(s_sm, smm.next())
            ss, sn = WK[0:NH, 7, 0:D], WK[0:NH, 7, D:D + NS]
            sw = ss.rearrange("p (w b q) -> p w b q", w=8, b=NS)
            sbw = ss.rearrange("p (w b q) -> p b w q", w=8, b=NS)
            mx, neg, es, den = (Z[0:NH, c:c + NS] for c in (384, 392, 400, 408))

            def wide(x):
                return x.unsqueeze(1).unsqueeze(3).broadcast_to((NH, 8, NS, 16))
            for b in range(NS):
                v.tensor_copy(sw[:, :, b, :], PS[0:NH, 4 + b // 4, (b % 4) * P:(b % 4 + 1) * P].rearrange("p (w q) -> p w q", w=8))
            v.tensor_copy(sn, PS[0:NH, 6, 0:NS]).then_inc(s_small, small.up())
            dve.wait_ge(s_small, small.at())
            v.tensor_reduce(mx, sbw, mybir.AxisListType.XY, ALU.max).then_inc(s_small, small.up())
            dve.wait_ge(s_small, small.at())
            v.tensor_tensor(mx, mx, sn, ALU.max).then_inc(s_small, small.up())
            dve.wait_ge(s_small, small.at())
            v.tensor_scalar(neg, mx, -SCALE, SINKC[:, 1:2], ALU.mult, ALU.min).then_inc(s_small, small.up())
            dve.wait_ge(s_small, small.at())
            v.tensor_scalar(WK[0:NH, 7, 0:D + NS], WK[0:NH, 7, 0:D + NS], SCALE, None, ALU.mult).then_inc(s_small, small.up())
            dve.wait_ge(s_small, small.at())
            svx = Count()
            v.tensor_tensor(sn, sn, neg, ALU.add).then_inc(s_small, small.up())
            dve.wait_ge(s_small, small.at())
            v.tensor_tensor(sw, sw, wide(neg), ALU.add).then_inc(s_svx, svx.up())
            dve.wait_ge(s_sa, sa.next())
            v.tensor_reduce(den, sbw, mybir.AxisListType.XY, ALU.add).then_inc(s_small, small.up())
            dve.wait_ge(s_small, small.at())
            v.tensor_tensor(den, den, es, ALU.add).then_inc(s_small, small.up())
            dve.wait_ge(s_small, small.at())
            v.tensor_tensor(den, den, sn, ALU.add).then_inc(s_small, small.up())
            dve.wait_ge(s_small, small.at())
            v.reciprocal(mx, den).then_inc(s_small, small.up())
            dve.wait_ge(s_small, small.at())
            v.tensor_tensor(sn, sn, mx, ALU.mult).then_inc(s_small, small.up())
            dve.wait_ge(s_small, small.at())
            v.tensor_tensor(sw, sw, wide(mx), ALU.mult).then_inc(s_sv, sv.up())
            dve.wait_ge(s_sm, smm.next())
            v.tensor_copy(Z[:, 416:416 + P], PS[:, 0, 0:P]).then_inc(s_small, small.up())
            dve.wait_ge(s_small, small.at())
            v.tensor_copy(Z[0:NS, 544:544 + NH], PS[0:NS, 0, P:P + NH]).then_inc(s_small, small.up())
            dve.wait_ge(s_small, small.at())
            pts = Z[:, 416:416 + P].rearrange("p (w h) -> p w h", w=8)
            for k in range(8):
                v.tensor_tensor(PBLK[:, k], pts[:, k, :].unsqueeze(1).broadcast_to((P, NS, NH)),
                                SEL.unsqueeze(2).broadcast_to((P, NS, NH)), ALU.mult)
            v.tensor_tensor(Z[0:NS, 256:256 + P].rearrange("p (b h) -> p b h", b=NS),
                                   Z[0:NS, 544:544 + NH].unsqueeze(1).broadcast_to((NS, NS, NH)),
                                   IDENT[0:NS, 0:NS].unsqueeze(2).broadcast_to((NS, NS, NH)), ALU.mult).then_inc(s_sv, sv.up())
            dve.wait_ge(s_sm, smm.next())
            for p in range(2):
                for hf in range(2):
                    rows, h0 = slice(hf * HD, (hf + 1) * HD), (2 * p + hf) * GROUP
                    src = PS[rows, 1, p * P:(p + 1) * P].rearrange("p (b h) -> p h b", b=NS)[:, h0:h0 + GROUP, :]
                    last = v.tensor_copy(QA[rows, p, :, SEQ:T], src)
            last.then_inc(s_sv, sv.up())
            dve.wait_ge(s_sv, sv.at())

        @block.vector
        def _(dve):
            own = Count()
            tr, trr = Count(), Count()
            mm, pr = Count(), Count()
            sq, acc = Count(), Count()
            hh, h = Count(), Count()
            tok, tokd, toka, dg = Count(), Count(), Count(), Count()
            bc, bcr = Count(), Count()
            v = nc.vector

            def side(s):
                return PS[:, 3 * s:3 * s + 3, 0:CH]

            def split_lo(m, x, gain=None):
                dve.wait_ge(s_hh, hh.next())
                if gain is None:
                    v.tensor_tensor(htile(1, m), x, htile(0, m).bitcast(F32), ALU.subtract).then_inc(s_h, h.up())
                else:
                    v.scalar_tensor_tensor(htile(1, m), x, gain, htile(0, m).bitcast(F32),
                                                 ALU.mult, ALU.subtract).then_inc(s_h, h.up())

            def split_x(row):
                with turns(dve, 0, KT, {hh: 1, h: 1}) as m:
                    split_lo(m, tile(X, m), par(m, row))

            def add_square(o):
                dve.wait_ge(s_sq, sq.next())
                dve.wait_ge(s_acc, acc.at())
                v.tensor_tensor(ACC, ACC, SQ[o], ALU.add).then_inc(s_acc, acc.up())

            def clear_acc():
                if tok.due():
                    dve.wait_ge(s_tok, tok.at())
                v.memset(ACC, 0.0).then_inc(s_acc, acc.up())

            def stat(norm, out):
                dve.wait_ge(s_tok, tok.next())
                t = TOK[:, 0, :]
                v.tensor_scalar(TOK[:, 0, 0:NB], PS[:, 6, 0:NB], 1.0 / D, EPS if norm else 0.0, ALU.mult, ALU.add).then_inc(s_v, own.up())
                dve.wait_ge(s_v, own.at())
                i = v.tensor_scalar(TOK[0:NS, 0, NB:NB + 1], PS[0:NS, 6, NB:NB + 1], 1.0 / D, EPS if norm else 0.0,
                                    ALU.mult, ALU.add)
                i.then_inc(s_tokd, tokd.up())
                dve.wait_ge(s_tokd, tokd.at())
                if norm:
                    dve.wait_ge(s_toka, toka.next())
                    t = TOK[:, 2, :]
                    v.reciprocal(t, TOK[:, 1, :]).then_inc(s_v, own.up())
                    dve.wait_ge(s_v, own.at())
                if out is None:
                    return
                dgb = DG[:, 0:SEQ].rearrange("p (b n) -> p b n", b=NB)
                v.tensor_tensor(dgb, IDENT.unsqueeze(1).broadcast_to((P, NB, P)), t[:, 0:NB].unsqueeze(2).broadcast_to((P, NB, P)), ALU.mult).then_inc(s_v, own.up())
                dve.wait_ge(s_v, own.at())
                v.tensor_scalar(DG[0:NS, SEQ:T], IDENT[0:NS, 0:NS], t[0:NS, NB:NB + 1], None, ALU.mult).then_inc(s_dg, dg.up())
                dve.wait_ge(s_bc, bc.next())
                v.tensor_copy(out[:, 0:BANK], PS[:, 6, :]).then_inc(s_bcr, bcr.up())
                v.tensor_copy(out[:, BANK:SEQ], PS[:, 7, :]).then_inc(s_bcr, bcr.up())
                dve.wait_ge(s_bc, bc.next())
                v.tensor_copy(out[:, SEQ:T], PS[:, 6, 0:NS]).then_inc(s_bcr, bcr.up())
                dve.wait_ge(s_bcr, bcr.at())

            def x_add(m, s, bias=None):
                dve.wait_ge(s_mm, mm.next())
                x = chunks(tile(X, m))
                if bias is None:
                    v.tensor_tensor(x, side(s), x, ALU.add).then_inc(s_pr, pr.up())
                else:
                    v.scalar_tensor_tensor(x, side(s), bias, x, ALU.add, ALU.add).then_inc(s_pr, pr.up())

            v.memset(TOK[:, :, :], 1.0).then_inc(s_v, own.up())
            dve.wait_ge(s_v, own.at())
            dve.wait_ge(s_tr, tr.next())
            v.tensor_copy(FPAR[:, 0:12, :].rearrange("p m r -> p (m r)"), PS[:, 5, 0:12 * 2 * NFR])
            v.tensor_copy(FPAR[:, 12:FT, :].rearrange("p m r -> p (m r)"), PS[:, 6, 0:10 * 2 * NFR])
            v.tensor_copy(X[:, :, SEQ:T], PS[:, 7, 0:KT * NS].rearrange("p (m n) -> p m n", m=KT))
            v.tensor_scalar(NSINK[:, :], PS[:, 7, 64:64 + NH], -1.0, None, ALU.mult).then_inc(s_acc, acc.up())
            v.tensor_scalar(SINKC[:, 1:2], SINKC[:, 0:1], -1.0, None, ALU.mult)
            v.tensor_copy(PAR[:, :, :].rearrange("p m r -> p (m r)"), PS[:, 0, 0:KT * NPAR]).then_inc(s_trr, trr.up())
            hst = WK[:, 7:9, 0:960]
            v.tensor_copy(hst.rearrange("p a (b n) -> p a b n", b=2),
                                  PS[:, 1:5, 0:480].rearrange("p (a b) n -> p a b n", a=2)).then_inc(s_trr, trr.up())
            clear_acc()
            with turns(dve, 0, KT // 2, {tr: 2, trr: 2, sq: 2, acc: 2}) as i:
                for o in range(2):
                    dve.wait_ge(s_tr, tr.next())
                    x = X[:, bass.ds(i * 2 + o, 1), 0:SEQ].rearrange("p a (c n) -> p (a c) n", c=2)
                    v.tensor_copy(x, PS[:, 2 * o:2 * o + 2, :]).then_inc(s_trr, trr.up())
                    add_square(o)
            acc_marks.append(acc.n)
            split_x(R_MIX)

            stat(True, RS)
            sig, glu, tap0, gh, gs, td, tt = (Count() for _ in range(7))
            GL, TA, TG, SIG, TM = (WK[:, k, :] for k in (4, 2, 3, 5, 6))
            sig.n = tap0.n = 1
            dve.wait_ge(s_taphi, 1)
            v.tensor_tensor(TAPLO, PAR[:, :, R_DW + CW - NT:R_DW + CW], TAPHI.bitcast(F32),
                            ALU.subtract).then_inc(s_taplo, 1)
            v.memset(GL[:, 0:HIST], 0.0).then_inc(s_v, own.up())
            dve.wait_ge(s_v, own.at())
            clear_acc()

            def conv_tile(q, o):
                i = q * 4 + o
                dve.wait_ge(s_mm, mm.next())
                dve.wait_ge(s_v, own.at())
                v.tensor_tensor(chunks(TA[:, 0:T]), side(0), chunks(RS), ALU.mult).then_inc(s_pr, pr.up())
                dve.wait_ge(s_mm, mm.next())
                dve.wait_ge(s_sig, sig.at())
                v.tensor_tensor(chunks(TG[:, 0:T]), side(1), chunks(RS), ALU.mult).then_inc(s_pr, pr.up())
                dve.wait_ge(s_sig, sig.next())
                dve.wait_ge(s_tap0, tap0.at())
                v.scalar_tensor_tensor(GL[:, HIST:WKC], TA[:, 0:T], par(i, R_B1), SIG[:, 0:T], ALU.add, ALU.mult).then_inc(s_glu, glu.up())
                n = NS * HIST
                hist = WK[:, bass.ds(q + 7, 1), o * n:(o + 1) * n].rearrange("p a b -> p (a b)")
                taps = par_taps(i)
                v.tensor_tensor(TM[:, 0:240].rearrange("p (b k) -> p b k", b=NS),
                                     hist.rearrange("p (b k) -> p b k", b=NS),
                                     taps.unsqueeze(1).broadcast_to((P, NS, HIST)), ALU.mult).then_inc(s_v, own.up())
                dve.wait_ge(s_v, own.at())
                v.tensor_reduce(TM[:, 240:248], TM[:, 0:240].rearrange("p (b k) -> p b k", b=NS), AX, ALU.add).then_inc(s_v, own.up())
                dve.wait_ge(s_v, own.at())
                dve.wait_ge(s_glu, glu.at())
                v.scalar_tensor_tensor(TM[:, 248:256], GL[:, HIST + SEQ:WKC], par(i, R_DW + HIST), TM[:, 240:248],
                                            ALU.mult, ALU.add).then_inc(s_v, own.up())
                dve.wait_ge(s_v, own.at())
                dve.wait_ge(s_gh, gh.next())
                v.tensor_tensor(GSPLIT[:, 1, 0:WKC], GL[:, 0:WKC], GSPLIT[:, 0, 0:WKC].bitcast(F32), ALU.subtract).then_inc(s_gs, gs.up())
                dve.wait_ge(s_tap0, tap0.next())
                v.tensor_scalar(tile(CONV, i, SEQ, T), TM[:, 248:256], par(i, R_BDW), None, ALU.add).then_inc(s_v, own.up())
                c = tile(CONV, i, 0, SEQ)
                for k in range(1, CW - NT):
                    v.scalar_tensor_tensor(c, GL[:, k:k + SEQ], par(i, R_DW + k), c, ALU.mult, ALU.add).then_inc(s_v, own.up())
                    dve.wait_ge(s_v, own.at())
                dve.wait_ge(s_td, td.next())
                c2 = CONV[:, bass.ds(i, 1), 0:SEQ].rearrange("p a (c n) -> p (a c) n", c=2)
                v.tensor_tensor(c2, PS[:, 6:8, :], c2, ALU.add).then_inc(s_tt, tt.up())
                dve.wait_ge(s_tt, tt.at())
                dve.wait_ge(s_acc, acc.at())
                v.tensor_tensor(ACC, ACC, tile(CONV, i), ALU.add).then_inc(s_acc, acc.up())

            def par_taps(i):
                if isinstance(i, int):
                    return PAR[:, i, R_DW:R_DW + HIST]
                return PAR[:, bass.ds(i, 1), R_DW:R_DW + HIST].rearrange("p a b -> p (a b)")

            with turns(dve, 0, KT // 4, {mm: 8, pr: 8, sig: 4, glu: 4, own: 4 * (4 + CW - 1 - NT), tap0: 4, acc: 4,
                                         gh: 4, gs: 4, td: 4, tt: 4}) as q:
                for o in range(4):
                    conv_tile(q, o)
            acc_marks.append(acc.n)
            MU = TG[:, 0:T]
            stat(False, MU)
            clear_acc()
            cen = Count()
            with turns(dve, 0, KT // 2, {cen: 2, sq: 2, acc: 2}) as i:
                for o in range(2):
                    c = tile(CONV, i * 2 + o)
                    v.tensor_tensor(c, c, MU, ALU.subtract).then_inc(s_conv, cen.up())
                    if o == 1:
                        for q in range(2):
                            dve.wait_ge(s_sq, sq.next())
                            dve.wait_ge(s_acc, acc.at())
                            v.tensor_tensor(ACC, ACC, LNSQ[q], ALU.add).then_inc(s_acc, acc.up())
            acc_marks.append(acc.n)
            stat(True, RS)
            y = Count()
            with turns(dve, 0, KT // 2, {cen: 2, y: 2, hh: 2, h: 2}) as i:
                for o in range(2):
                    c = tile(CONV, i * 2 + o)
                    v.tensor_tensor(c, c, RS, ALU.mult).then_inc(s_conv, cen.up())
                for o in range(2):
                    y.n += 1
                    dve.wait_ge(s_hh, hh.next())
                    v.tensor_tensor(htile(1, i * 2 + o), LNSQ[o], htile(0, i * 2 + o).bitcast(F32), ALU.subtract).then_inc(s_h, h.up())
            clear_acc()
            with turns(dve, 0, KT // 2, {mm: 2, pr: 2, sq: 2, acc: 2}) as i:
                for o in range(2):
                    x_add(i * 2 + o, o, par(i * 2 + o, R_B2))
                    add_square(o)
            acc_marks.append(acc.n)

            g_, t2, gc, silu, m_, mh, mid = (Count() for _ in range(7))
            silu.n = y.n
            GB, TT, MM = WK[:, 4, :], WK[:, 5, 0:T], WK[:, 6, 0:T]

            def ffn(l):
                split_x(R_FFN + l)
                stat(True, RS)
                base = l * NFR
                v.memset(GB[:, 0:2], 0.0).then_inc(s_v, own.up())
                dve.wait_ge(s_v, own.at())

                def gate(s, f, adds=()):
                    dve.wait_ge(s_mm, mm.next())
                    if t2.due():
                        dve.wait_ge(s_t2, t2.at())
                    v.tensor_tensor(chunks(GB[:, 2:2 + T]), side(s), chunks(RS), ALU.mult).then_inc(s_pr, pr.up())
                    dve.wait_ge(s_t2, t2.next())
                    t = TT[:, 0:SEQ]
                    v.scalar_tensor_tensor(t, GB[:, 1:1 + SEQ], fpar(f, base + FR_W + 1), t, ALU.mult, ALU.add).then_inc(s_v, own.up())
                    if 0 in adds:
                        x_add(0, 1)
                    dve.wait_ge(s_v, own.at())
                    v.scalar_tensor_tensor(t, GB[:, 0:SEQ], fpar(f, base + FR_W), t, ALU.mult, ALU.add).then_inc(s_v, own.up())
                    if 1 in adds:
                        x_add(1, 0)
                    dve.wait_ge(s_v, own.at())
                    t = TT[:, SEQ:T]
                    st = fpar(f, base + FR_ST, 2 * NS).rearrange("p (b j) -> p j b", j=2)
                    v.scalar_tensor_tensor(t, st[:, 1, :], fpar(f, base + FR_W + 1), t, ALU.mult, ALU.add).then_inc(s_v, own.up())
                    dve.wait_ge(s_v, own.at())
                    v.scalar_tensor_tensor(t, st[:, 0, :], fpar(f, base + FR_W), t, ALU.mult, ALU.add).then_inc(s_gc, gc.up())

                def value(s, q):
                    dve.wait_ge(s_silu, silu.next())
                    dve.wait_ge(s_mm, mm.next())
                    if mh.due():
                        dve.wait_ge(s_mh, mh.at())
                    dve.wait_ge(s_v, own.at())
                    v.tensor_tensor(chunks(MM), side(s), chunks(TT), ALU.mult).then_inc(s_pr, pr.up())
                    dve.wait_ge(s_pr, pr.at())
                    v.tensor_tensor(MM, MM, RS, ALU.mult).then_inc(s_m, m_.up())
                    dve.wait_ge(s_mh, mh.next())
                    v.tensor_tensor(MID[:, q, 1, :], MM, MID[:, q, 0, :].bitcast(F32), ALU.subtract).then_inc(s_mid, mid.up())

                gate(0, 0)
                value(1, 0)
                gate(0, 1)
                value(1, 1)
                with turns(dve, 1, FT // 2, {mm: 12, pr: 12, t2: 2, own: 6, gc: 2, silu: 2, m_: 2, mh: 2, mid: 2}) as i:
                    gate(0, i * 2, adds=(0, 1))
                    for m in range(2, KT):
                        x_add(m, (m + 1) % 2)
                    value(1, 0)
                    gate(0, i * 2 + 1)
                    value(1, 1)
                clear_acc()
                with turns(dve, 0, KT // 2, {mm: 2, pr: 2, sq: 2, acc: 2}) as i:
                    for o in range(2):
                        x_add(i * 2 + o, (o + 1) % 2)
                        add_square(o)
                acc_marks.append(acc.n)
            ffn(0)

            heads = Count()
            split_x(R_MIX + 1)
            stat(True, RS)
            for j in range(2):
                dve.wait_ge(s_mm, mm.next())
                v.tensor_tensor(chunks(WK[:, 4 + j, 0:T]), side(j), chunks(RS), ALU.mult).then_inc(s_pr, pr.up())
            dve.wait_ge(s_tab, 16)
            v.tensor_tensor(COS, COS, RS, ALU.mult).then_inc(s_v, own.up())
            dve.wait_ge(s_v, own.at())
            v.tensor_tensor(SIN, SIN, RS, ALU.mult).then_inc(s_v, own.up())
            dve.wait_ge(s_v, own.at())

            def raw_heads(s, t):
                dve.wait_ge(s_mm, mm.next())
                if heads.due():
                    dve.wait_ge(s_heads, heads.at())
                v.tensor_copy(chunks(WK[:, 1 + t % 2, 0:T]), side(s)).then_inc(s_pr, pr.up())

            def turn_heads(s, t):
                R = WK[:, 1 + t % 2, 0:T]
                T1 = WK[:, 3, 0:T]
                if heads.due():
                    dve.wait_ge(s_heads, heads.at())
                dve.wait_ge(s_pr, pr.at())
                v.tensor_tensor(T1, R, COS, ALU.mult).then_inc(s_v, own.up())
                dve.wait_ge(s_mm, mm.next())
                dve.wait_ge(s_v, own.at())
                v.tensor_tensor(chunks(R), side(s), chunks(SIN), ALU.mult).then_inc(s_pr, pr.up())
                dve.wait_ge(s_pr, pr.at())
                if t < 2:
                    v.tensor_tensor(WK[:, K_TILE[t], 0:T], T1, R, ALU.add).then_inc(s_heads, heads.up())
                    return
                q = t - 2
                j = q // 2
                rows = slice((j % 2) * HD, (j % 2 + 1) * HD)
                for o in range(2):
                    src = slice(o * HD, (o + 1) * HD)
                    v.tensor_tensor(QA[rows, j // 2, 2 * (q % 2) + o, :], T1[src, :], R[src, :], ALU.add).then_inc(s_heads, heads.up())

            raw_heads(0, 0)
            raw_heads(1, 1)
            for t in range(KT):
                turn_heads(0, t)
                raw_heads(1, t)
            turn_heads(0, KT)
            turn_heads(1, KT + 1)
            assert heads.n == HEADS

            attention_dve(dve)

            qt = QA[:, :, :, :].rearrange("p a g n -> p (a g) n")
            with turns(dve, 0, KT, {hh: 1, h: 1}) as m:
                split_lo(m, tile(qt, m))
            clear_acc()
            with turns(dve, 0, KT // 2, {mm: 2, pr: 2, sq: 2, acc: 2}) as i:
                for o in range(2):
                    x_add(i * 2 + o, o)
                    add_square(o)
            acc_marks.append(acc.n)
            ffn(1)

            stat(True, None)
            dve.wait_ge(s_v, own.at())
            dve.wait_ge(s_tr, tr.next())
            v.tensor_copy(WK[0:HIST + NS, 5, 0:D], PS[0:HIST + NS, 0:2, :].rearrange("p a n -> p (a n)")).then_inc(s_trr, trr.up())
            for l in range(2):
                for part in range(2):
                    dve.wait_ge(s_tr, tr.next())
                    n = FT // 2 * P
                    dst = GROWS[l][0:2 + NS, part * n:(part + 1) * n]
                    src = PS[0:2 + NS, 2:5, :].rearrange("p a n -> p (a n)")[:, 0:n]
                    v.tensor_copy(dst, src).then_inc(s_trr, trr.up())
            with turns(dve, 0, NB // 2, {tr: 2, trr: 2}) as i:
                for o in range(2):
                    dve.wait_ge(s_tr, tr.next())
                    dst = YOUT[:, bass.ds(i * 2 + o, 1), :].rearrange("p a (c n) -> p (a c) n", c=2)
                    v.tensor_scalar(dst, PS[:, 2 * o:2 * o + 2, :],
                                            TOK[:, 2, bass.ds(i * 2 + o, 1)], None, ALU.mult).then_inc(s_trr, trr.up())
            dve.wait_ge(s_tr, tr.next())
            v.tensor_scalar(WK[0:NS, 4, 0:D], PS[0:NS, 0:2, :].rearrange("p a n -> p (a n)"),
                                    TOK[0:NS, 2, NB:NB + 1], None, ALU.mult).then_inc(s_trr, trr.up())

        @block.scalar
        def _(act):
            sc_ = nc.scalar
            act.dma_start(CST[:, :], a["const_small"]).then_inc(s_const, 16)
            r = lambda k, n=1: WK[k:k + n, 0, 0:D]
            rows = [(r(R_MIX, 2), a["norm_mix"]), (r(R_FFN, 2), a["norm_ffn"]),
                    (r(R_FIN), a["norm_final"].rearrange("(a n) -> a n", a=1)),
                    (r(R_B1, 2), a["conv_b_pw1"].rearrange("a (b n) -> (a b) n", b=2)),
                    (r(R_DW, CW), a["conv_w_dw"][0]), (r(R_BDW), a["conv_b_dw"]), (r(R_LNG), a["conv_ln_g"]),
                    (r(R_LNB), a["conv_ln_b"]), (r(R_B2), a["conv_b_pw2"]),
                    (WK[0:NS, 3, 0:D], a["x_sample"].rearrange("b s d -> (b s) d")),
                    (WK[0:1, 3, D:D + NH], a["attn_sinks"]), (SINKC[:, 0:1], a["attn_sinks"].rearrange("a h -> h a"))]
            hist = a["state_conv"].rearrange("a b k d -> (a b k) d")
            frow = WK[:, 4:7, :].rearrange("p a n -> p (a n)")
            half = NS * HIST // 2
            rows += [(WK[0:half, 1, 0:D], hist[0:half]), (WK[0:half, 2, 0:D], hist[half:2 * half])]
            fr = []
            for l in range(2):
                b = l * NFR
                fr += [(frow[b + FR_W:b + FR_B, 0:F], a["ffn_w_dw"][l]),
                       (frow[b + FR_B:b + FR_ST, 0:F], a["ffn_b_dw"][l:l + 1]),
                       (frow[b + FR_ST:b + NFR, 0:F], a["state_ffn"][l].rearrange("b k f -> (b k) f"))]
            assert len(rows) + len(fr) == ROW_DMAS
            for dst, src in rows + fr:
                act.dma_start(dst, src).then_inc(s_rows, 16)
            for b in range(NB):
                act.dma_start(XIN[:, b, :], a["x_prompt"][0, b * P:(b + 1) * P, :]).then_inc(s_x, 16)
            act.dma_start(a["new_conv_sample"][0, :, 0:HIST - 1, :], a["state_conv"][0, :, 1:HIST, :]).then_inc(s_st, 16)
            act.dma_start(a["new_ffn_sample"][:, :, 0, :], a["state_ffn"][:, :, 1, :]).then_inc(s_st, 16)
            for new, old in (("new_k_sample", "cache_k"), ("new_v_sample", "cache_v")):
                act.dma_start(a[new][0, :, 0:WIN - 1].rearrange("b w j d -> b (w j d)"),
                              a[old][0, :, 1:WIN].rearrange("b w j d -> b (w j d)")).then_inc(s_st, 16)

            own = Count()
            trr, pr, sq, acc = Count(), Count(), Count(), Count()
            hh, h, tokd, toka = Count(), Count(), Count(), Count()
            F_ = sc_.activation

            def square(src, dst, reader_back=1):
                act.wait_ge(s_acc, acc.at(reader_back))
                acc.n += 1
                F_(dst, src, ACT.Square).then_inc(s_sq, sq.up())

            def root():
                act.wait_ge(s_tokd, tokd.next())
                F_(TOK[:, 1, :], TOK[:, 0, :], ACT.Sqrt).then_inc(s_toka, toka.up())

            def split_x(row):
                with turns(act, 0, KT, {hh: 1}) as m:
                    F_(htile(0, m), tile(X, m), ACT.Identity, scale=par(m, row)).then_inc(s_hh, hh.up())

            def residual_squares():
                acc.n += 1
                with turns(act, 0, KT // 2, {pr: 2, acc: 2, sq: 2}) as i:
                    for o in range(2):
                        act.wait_ge(s_pr, pr.next())
                        square(tile(X, i * 2 + o), SQ[o])

            trr.n += 2
            acc.n += 2
            with turns(act, 0, KT // 2, {trr: 2, acc: 2, sq: 2}) as i:
                for o in range(2):
                    act.wait_ge(s_trr, trr.next())
                    square(tile(X, i * 2 + o), SQ[o])
            split_x(R_MIX)
            root()
            sig, glu, tap0, gh, diag, td = (Count() for _ in range(6))

            def diagonals(i, D_, first):
                for k in range(D_.shape[2]):
                    F_(D_[:, 0, k, :], IDENT, ACT.Identity, scale=par(i, R_DW + CW - NT + first + k))
                    lo = TAPLO[:, bass.ds(i, 1), first + k:first + k + 1].rearrange("p a b -> p (a b)")
                    last = F_(D_[:, 1, k, :], IDENT, ACT.Identity, scale=lo)
                last.then_inc(s_diag, diag.up())
            GL, TG, SIG = (WK[:, k, :] for k in (4, 3, 5))
            act.sem_inc(s_sig, 1)
            act.sem_inc(s_tap0, 1)
            F_(TAPHI, PAR[:, :, R_DW + CW - NT:R_DW + CW], ACT.Copy).then_inc(s_taphi, 1)
            act.wait_ge(s_taplo, 1)
            diagonals(0, DIAGA, 0)

            def conv_act(i):
                act.wait_ge(s_pr, pr.next(2))
                F_(SIG[:, 0:T], TG[:, 0:T], ACT.Sigmoid, bias=par(i, R_B1 + 1)).then_inc(s_sig, sig.up())
                act.wait_ge(s_glu, glu.next())
                F_(GSPLIT[:, 0, 0:WKC], GL[:, 0:WKC], ACT.Copy).then_inc(s_gh, gh.up())
                diagonals(i, DIAGB, NTA)
                F_(tile(CKEEP, i, 0, HIST + NS), GL[:, SEQ:WKC], ACT.Copy)
                F_(tile(CONV, i, 0, SEQ), GL[:, 0:SEQ], ACT.Identity, scale=par(i, R_DW), bias=par(i, R_BDW)).then_inc(s_tap0, tap0.up())

            with turns(act, 0, KT - 1, {pr: 2, sig: 1, glu: 1, tap0: 1, gh: 1, diag: 2, td: 1}) as i:
                conv_act(i)
                act.wait_ge(s_td, td.next())
                diagonals(i + 1, DIAGA, 0)
            conv_act(KT - 1)
            acc.n += 1 + KT
            tokd.n += 1
            cen = Count()
            acc.n += 1
            with turns(act, 0, KT // 2, {cen: 2, acc: 2, sq: 2}) as i:
                for o in range(2):
                    act.wait_ge(s_conv, cen.next())
                    square(tile(CONV, i * 2 + o), LNSQ[o])
            root()
            act.dma_start(WK[:, 7:9, 0:T], a["const_rope"].rearrange("p (a n) -> p a n", a=2)).then_inc(s_tab, 16)
            y = Count()
            h.n = KT
            with turns(act, 0, KT // 2, {cen: 2, h: 2, hh: 2, y: 2}) as i:
                for o in range(2):
                    act.wait_ge(s_conv, cen.next())
                    act.wait_ge(s_h, h.at(1))
                    h.n += 1
                    F_(LNSQ[o], tile(CONV, i * 2 + o), ACT.Silu, scale=par(i * 2 + o, R_LNG), bias=par(i * 2 + o, R_LNB)).then_inc(s_silu, y.up())
                    act.wait_ge(s_silu, y.at())
                    F_(htile(0, i * 2 + o), LNSQ[o], ACT.Copy).then_inc(s_hh, hh.up())
            residual_squares()

            t2, gc, silu, m_, mh = (Count() for _ in range(5))
            silu.n = y.n
            GB, TT, MM = WK[:, 4, :], WK[:, 5, 0:T], WK[:, 6, 0:T]

            def ffn(l):
                split_x(R_FFN + l)
                root()
                base = l * NFR

                def gate(f):
                    act.wait_ge(s_pr, pr.next())
                    F_(tile(GKEEP[:, l], f, 0, 2 + NS), GB[:, SEQ:2 + T], ACT.Copy)
                    F_(TT, GB[:, 2:2 + T], ACT.Identity, scale=fpar(f, base + FR_W + 2), bias=fpar(f, base + FR_B)).then_inc(s_t2, t2.up())
                    act.wait_ge(s_gc, gc.next())
                    F_(TT, TT, ACT.Silu).then_inc(s_silu, silu.up())

                def value(q):
                    pr.n += 1
                    act.wait_ge(s_m, m_.next())
                    F_(MID[:, q, 0, :], MM, ACT.Copy).then_inc(s_mh, mh.up())

                gate(0)
                value(0)
                gate(1)
                value(1)
                with turns(act, 1, FT // 2, {pr: 12, t2: 2, gc: 2, silu: 2, m_: 2, mh: 2}) as i:
                    gate(i * 2)
                    pr.n += KT
                    value(0)
                    gate(i * 2 + 1)
                    value(1)
                residual_squares()
            ffn(0)

            split_x(R_MIX + 1)
            root()
            act.wait_ge(s_heads, HEADS)
            act.dma_start(WK[:, 7, 0:D], a["const_mask"]).then_inc(s_tab, 16)
            kvh = Count()
            for p in range(2):
                F_(KR[:, 0, p, P:PADK], WK[:, K_TILE[p], 0:T], ACT.Copy).then_inc(s_kvh, kvh.up())
            F_(IDR[:, :], IDENT, ACT.Copy).then_inc(s_kvh, kvh.up())
            act.wait_ge(s_tab, 32)
            F_(MASK[:, :, :].rearrange("p a n -> p (a n)"), WK[:, 7, 0:D], ACT.Copy).then_inc(s_kvh, kvh.up())
            act.wait_ge(s_kvr, 1)
            F_(VR[:, 0, 1:NB + 1, :].rearrange("p (a b) n -> p a (b n)", b=2), PS[:, 0:4, :], ACT.Copy).then_inc(s_kvh, kvh.up())
            act.wait_ge(s_kv, KV_READY)
            kn, vn = a["new_k_prompt"], a["new_v_prompt"]
            act.dma_start(kn[0, 0].rearrange("w j d -> w (j d)"), WK[:, 8, BANK:BANK + 256]).then_inc(s_st, 16)
            act.dma_start(vn[0, 0].rearrange("w j d -> w (j d)"), WK[:, 8, BANK + 256:2 * BANK]).then_inc(s_st, 16)
            for c, new in ((0, "new_v_sample"), (256, "new_k_sample")):
                act.dma_start(a[new][0, :, WIN - 1].rearrange("b j d -> b (j d)"), WK[0:NS, 8, c:c + 256]).then_inc(s_st, 16)
            for c, old in ((0, "cache_k"), (2, "cache_v")):
                src = a[old][0].rearrange("b (q w) j d -> (b q) (w j d)", q=16)
                act.dma_start(WK[:, c:c + 2, 0:D], src.rearrange("p (a n) -> p a n", a=2)).then_inc(s_cache, 16)
            qh, sc, nm, ex = Count(), Count(), Count(), Count()
            pt, pth, pv, ov = Count(), Count(), Count(), Count()

            def q_hi(n, p):
                if n > 0:
                    act.wait_ge(s_sc, 4 * (n - 1) + 2 * p + 2)
                F_(QS[:, p, 0, :].rearrange("p (g n) -> p g n", g=GROUP), QA[:, p, :, n * P:(n + 1) * P], ACT.Copy).then_inc(s_qh, qh.up())

            def exps(n, p, hf):
                j = 2 * p + hf
                act.wait_ge(s_nm, nm.next(2))
                for g in range(GROUP):
                    F_(PX[:, hf, g, :], PS[:, 2 * hf + g // 2, (g % 2) * 256:(g % 2 + 1) * 256], ACT.Exp,
                       scale=SCALE, bias=SMALL[:, hf, 1, g:g + 1], accum_out=SMALL[:, hf, 3, g:g + 1])
                F_(SMALL[:, hf, 4, :], SMALL[:, hf, 2, :], ACT.Exp).then_inc(s_ex, ex.up())

            q_hi(0, 0)
            exps(*UNITS[0])
            for u, (n, p, hf) in enumerate(UNITS):
                if u + 2 < len(UNITS) and UNITS[u + 2][2] == 0:
                    q_hi(*UNITS[u + 2][:2])
                act.wait_ge(s_pt, pt.next())
                F_(PT[:, 0], PS[:, 4:6, :], ACT.Copy).then_inc(s_pth, pth.up())
                if u + 1 < len(UNITS):
                    exps(*UNITS[u + 1])
                act.wait_ge(s_pv, pv.next())
                rows_ = slice(hf * HD, (hf + 1) * HD)
                F_(QA[rows_, p, :, n * P:(n + 1) * P],
                          PS[rows_, 6 + hf, :].rearrange("p (g n) -> p g n", g=GROUP), ACT.Copy).then_inc(s_ov, ov.up())
            sa = Count()
            act.wait_ge(s_svx, 1)
            ss = WK[0:NH, 7, 0:D + NS]
            F_(WK[0:NH, 6, 400:408], WK[0:NH, 6, 392:400], ACT.Exp, bias=SINKC[:, 0:1])
            F_(ss, ss, ACT.Exp).then_inc(s_sa, sa.up())
            act.wait_ge(s_sv, 5)
            qt = QA[:, :, :, :].rearrange("p a g n -> p (a g) n")
            with turns(act, 0, KT, {hh: 1}) as m:
                F_(htile(0, m), tile(qt, m), ACT.Copy).then_inc(s_hh, hh.up())
            pr.n += 12 + KT + 2
            residual_squares()
            ffn(1)

            xg = Count()
            act.wait_ge(s_acc, acc.at())
            for m in range(KT):
                F_(X[:, m, :], X[:, m, :], ACT.Identity, scale=par(m, R_FIN)).then_inc(s_xg, xg.up())
            root()
            trr.n = 2 + KT
            act.wait_ge(s_trr, trr.next(5))
            act.dma_start(a["new_conv_prompt"][0, 0], WK[0:HIST, 5, 0:D]).then_inc(s_st, 16)
            act.dma_start(a["new_conv_sample"][0, :, HIST - 1, :], WK[HIST:HIST + NS, 5, 0:D]).then_inc(s_st, 16)
            for l in range(2):
                act.dma_start(a["new_ffn_prompt"][l, 0], GROWS[l][0:2, 0:F]).then_inc(s_st, 16)
                act.dma_start(a["new_ffn_sample"][l, :, 1, :], GROWS[l][2:2 + NS, 0:F]).then_inc(s_st, 16)

        def attention_pe(pe, transpose, PASSES):
            matmul = nc.tensor.matmul
            kv, qs, sc, ex = Count(), Count(), Count(), Count()
            pn, pt, ptl = Count(), Count(), Count()
            pv, ov = Count(), Count()
            smm, sdv = Count(), Count()
            pe.wait_ge(s_heads, HEADS)
            for j in range(2):
                for b in range(NB):
                    transpose(PS[:, b // 2, (b % 2) * 256 + j * P:(b % 2) * 256 + (j + 1) * P],
                              WK[:, 4 + j, b * P:(b + 1) * P])
                transpose(PS[0:NS, 4, j * P:(j + 1) * P], WK[:, 4 + j, SEQ:T])
                kt = WK[:, K_TILE[j], :]
                transpose(PS[:, 5, j * P:(j + 1) * P], kt[:, SEQ - P:SEQ])
                last = transpose(PS[0:NS, 4, (2 + j) * P:(3 + j) * P], kt[:, SEQ:T])
            last.then_inc(s_kvo, 1)
            pe.wait_ge(s_kv, kv.next(KV_READY))

            def scores(n, p, hf):
                if hf == 0:
                    pe.wait_ge(s_qs, qs.next())
                if ex.due(1):
                    pe.wait_ge(s_ex, ex.at(1))
                ex.n += 1
                rows = slice(hf * HD, (hf + 1) * HD)
                first = 0 if n == 0 else 1
                for b in range(2):
                    for g in (2 * b, 2 * b + 1):
                        for q, (kp, qp) in enumerate(PASSES):
                            out = PS[:, 2 * hf + b, (g % 2) * 256:(g % 2 + 1) * 256]
                            matmul(out, QS[rows, p, qp, g * P:(g + 1) * P],
                                   KR[rows, kp, p, n * P:n * P + 2 * P],
                                   start=(g % 2 == 0 and q == 0), stop=False, skip_group_check=True)
                    last = matmul(PS[:, 2 * hf + b, :], IDR[:, :], MASK[:, first, :], start=False, stop=True,
                                  skip_group_check=True)
                last.then_inc(s_sc, sc.up())

            def heads(n, p, hf):
                pe.wait_ge(s_pn, pn.next())
                if ptl.due():
                    pe.wait_ge(s_ptl, ptl.at())
                ptl.n += 1
                for s in range(2):
                    for g in range(GROUP):
                        last = transpose(PS[:, 4 + s, g * P:(g + 1) * P], PX[:, hf, g, s * P:(s + 1) * P])
                last.then_inc(s_pt, pt.up())
                if ov.due(1):
                    pe.wait_ge(s_ov, ov.at(1))
                ov.n += 1
                if ptl.due():
                    pe.wait_ge(s_ptl, ptl.at())
                for s in range(2):
                    vb = VR[:, :, n + s, p * P:(p + 1) * P]
                    for q, (vp, pp) in enumerate(PASSES):
                        last = matmul(PS[:, 6 + hf, :], vb[:, vp, :], PT[:, pp, s, :],
                                      start=(s == 0 and q == 0), stop=(s == 1 and q == 2))
                last.then_inc(s_pv, pv.up())

            scores(*UNITS[0])
            for u in range(len(UNITS)):
                if u + 1 < len(UNITS):
                    scores(*UNITS[u + 1])
                heads(*UNITS[u])

            pe.wait_ge(s_ov, ov.at())
            pe.wait_ge(s_cache, 32)
            for p in range(2):
                for k in range(NS):
                    last = transpose(PS[:, 2 * p + k // 4, (k % 4) * P:(k % 4 + 1) * P],
                                     WK[:, 0:2, 0:D][:, k // 4, (k % 4) * 256 + p * P:(k % 4) * 256 + (p + 1) * P])
            last.then_inc(s_sm, smm.up())
            pe.wait_ge(s_sv, sdv.next(2))
            kct = WK[:, 4:6, 0:D].rearrange("p a (w r) -> p a w r", w=8)
            for b in range(NS):
                for p in range(2):
                    qb = WK[:, 6, 0:256].rearrange("p (a b h) -> p a b h", a=2, b=NS)[:, p, b, :]
                    matmul(PS[0:NH, 4 + b // 4, (b % 4) * P:(b % 4 + 1) * P], qb,
                           kct[:, p, :, b * 16:(b + 1) * 16], start=(p == 0), stop=(p == 1))
            for b in range(NS):
                for p in range(2):
                    qb = WK[:, 6, 0:256].rearrange("p (a b h) -> p a b h", a=2, b=NS)[:, p, b, :]
                    last = matmul(PS[0:NH, 6, b:b + 1], qb, WK[:, K_TILE[p], SEQ + b:SEQ + b + 1], start=(p == 0), stop=(p == 1))
            last.then_inc(s_sm, smm.up())
            pe.wait_ge(s_sv, sdv.next())
            for k in range(8):
                transpose(PS[:, 0, k * NH:(k + 1) * NH], WK[0:NH, 7, k * P:(k + 1) * P])
            last = transpose(PS[0:NS, 0, P:P + NH], WK[0:NH, 7, D:D + NS])
            last.then_inc(s_sm, smm.up())
            pe.wait_ge(s_sv, sdv.next())
            pnb = WK[0:NS, 6, 256:256 + P]
            for p in range(2):
                for k in range(8):
                    matmul(PS[:, 1, p * P:(p + 1) * P], WK[:, 2 + k // 4, (k % 4) * 256 + p * P:(k % 4) * 256 + (p + 1) * P],
                           PBLK[:, k, :, :].rearrange("p b h -> p (b h)"), start=(k == 0), stop=False)
                last = matmul(PS[:, 1, p * P:(p + 1) * P], WK[0:NS, 8, p * P:(p + 1) * P], pnb, start=False, stop=True)
            last.then_inc(s_sm, smm.up())
            pe.wait_ge(s_sv, sdv.next())

        @block.tensor
        def _(pe):
            tr, trr = Count(), Count()
            mm, pr = Count(), Count()
            w, started = Count(), Count()
            h = Count()
            acc = Count()
            tok, tokd, dg = Count(), Count(), Count()
            bc, bcr = Count(), Count()
            mid = Count()
            matmul = nc.tensor.matmul
            PASSES = ((0, 0), (0, 1), (1, 0))

            def begin_group():
                if pr.due(1):
                    pe.wait_ge(s_pr, pr.at(1))
                pr.n += 1

            def dense(side, slot, wait_h=False, after=None, hook=None):
                pe.wait_ge(s_w, w.next())
                begin_group()
                for k in range(KT):
                    if wait_h:
                        pe.wait_ge(s_h, h.next())
                    for q, (wp, hp) in enumerate(PASSES):
                        for c in range(NCH):
                            last = matmul(PS[:, 3 * side + c, 0:CH], W[:, slot, wp, k * P:(k + 1) * P],
                                          H[:, hp, k, c * CH:(c + 1) * CH],
                                          start=(k == 0 and q == 0), stop=(k == KT - 1 and q == 2))
                            if k == 0 and q == 0 and c == 0:
                                last.then_inc(s_wstart, started.up())
                    if hook and k == after:
                        hook()
                last.then_inc(s_mm, mm.up())

            def down(slot):
                pe.wait_ge(s_w, w.next())
                for m in range(4):
                    begin_group()
                    side = (m + 1) % 2
                    for t in range(2):
                        for q, (wp, hp) in enumerate(PASSES):
                            for c in range(NCH):
                                last = matmul(PS[:, 3 * side + c, 0:CH],
                                              W[:, slot, wp, t * BANK + m * P:t * BANK + (m + 1) * P],
                                              MID[:, t, hp, c * CH:(c + 1) * CH],
                                              start=(t == 0 and q == 0), stop=(t == 1 and q == 2))
                                if m == 0 and t == 0 and q == 0 and c == 0:
                                    last.then_inc(s_wstart, started.up())
                    last.then_inc(s_mm, mm.up())

            def token_sums(accs):
                acc.n = accs
                pe.wait_ge(s_acc, acc.at())
                for b in range(NB + 1):
                    n = P if b < NB else NS
                    last = matmul(PS[0:n, 6, b:b + 1], ACC[:, b * P:b * P + n], ONES[:, 0:1], start=True, stop=True)
                last.then_inc(s_tok, tok.up())

            def broadcast():
                pe.wait_ge(s_dg, dg.next())
                matmul(PS[:, 6, :], ONES, DG[:, 0:BANK], start=True, stop=True)
                matmul(PS[:, 7, :], ONES, DG[:, BANK:SEQ], start=True, stop=True).then_inc(s_bc, bc.up())
                pe.wait_ge(s_bcr, bcr.next())
                matmul(PS[:, 6, 0:NS], ONES[0:NS, :], DG[0:NS, SEQ:T], start=True, stop=True).then_inc(s_bc, bc.up())
                bcr.n += 2

            def transpose(out, in_):
                n = in_.shape[0]
                return nc.tensor.transpose(out, in_, IDENT[0:n, 0:n])

            pe.wait_ge(s_const, 16)
            pe.wait_ge(s_rows, 16 * ROW_DMAS)
            for m in range(KT):
                last = transpose(PS[:, 0, m * NPAR:(m + 1) * NPAR], WK[0:NPAR, 0, m * P:(m + 1) * P])
                for hf in range(2):
                    rows = HIST * NS // 2
                    last = transpose(PS[:, 1 + m // 2, (m % 2) * 240 + hf * rows:(m % 2) * 240 + (hf + 1) * rows],
                                     WK[0:rows, 1 + hf, m * P:(m + 1) * P])
            for f in range(FT):
                rows = WK[0:2 * NFR, 4:7, :].rearrange("p a n -> p (a n)")
                last = transpose(PS[:, 5 + f // 12, (f % 12) * 2 * NFR:(f % 12 + 1) * 2 * NFR], rows[:, f * P:(f + 1) * P])
            for m in range(KT):
                last = transpose(PS[:, 7, m * NS:(m + 1) * NS], WK[0:NS, 3, m * P:(m + 1) * P])
            last = matmul(PS[:, 7, 64:64 + NH], ONES[0:1, :], WK[0:1, 3, D:D + NH], start=True, stop=True)
            last.then_inc(s_tr, tr.up())
            pe.wait_ge(s_trr, trr.next(2))
            pe.wait_ge(s_x, 16 * NB)
            for m in range(KT):
                o = m % 2
                pe.wait_ge(s_trr, trr.at(1))
                trr.n += 1
                for b in range(NB):
                    last = transpose(PS[:, 2 * o + b // 4, (b % 4) * P:(b % 4 + 1) * P], XIN[:, b, m * P:(m + 1) * P])
                last.then_inc(s_tr, tr.up())
            pe.wait_ge(s_trr, trr.at())

            ACCS = iter(acc_marks)
            dense(0, 0, wait_h=True)
            token_sums(next(ACCS))
            dense(1, 1, after=3, hook=broadcast)
            gs, diag, td, tt = (Count() for _ in range(4))

            def last_taps():
                pe.wait_ge(s_diag, diag.next(2))
                pe.wait_ge(s_gs, gs.next())
                if tt.due():
                    pe.wait_ge(s_tt, tt.at())
                tt.n += 1
                for k in range(NT):
                    diagonal = DIAGA[:, :, k, :] if k < NTA else DIAGB[:, :, k - NTA, :]
                    for q, (wp, gp) in enumerate(PASSES):
                        for c in range(2):
                            col = CW - NT + k + c * BANK
                            last = matmul(PS[:, 6 + c, :], diagonal[:, wp, :], GSPLIT[:, gp, col:col + BANK],
                                          start=(k == 0 and q == 0), stop=(k == NT - 1 and q == 2))
                last.then_inc(s_td, td.up())
            dense(0, 0)
            last_taps()
            dense(1, 1)
            with turns(pe, 2, KT, {w: 2, started: 2, mm: 2, pr: 2, gs: 1, diag: 2, td: 1, tt: 1}):
                dense(0, 0)
                last_taps()
                dense(1, 1)
            last_taps()
            token_sums(next(ACCS))
            broadcast()
            token_sums(next(ACCS))
            broadcast()
            dense(0, 0, wait_h=True)
            dense(1, 1)
            with turns(pe, 1, KT // 2, {w: 2, started: 2, mm: 2, pr: 2}):
                dense(0, 0)
                dense(1, 1)

            def ffn():
                dense(0, 0, wait_h=True)
                token_sums(next(ACCS))
                dense(1, 1, after=3, hook=broadcast)
                dense(0, 0)
                dense(1, 1)
                with turns(pe, 1, FT // 2, {w: 6, started: 6, mm: 12, pr: 12, mid: 2}):
                    dense(0, 0)
                    pe.wait_ge(s_mid, mid.next(2))
                    down(1)
                    down(0)
                    dense(1, 1)
                    dense(0, 0)
                    dense(1, 1)
                pe.wait_ge(s_mid, mid.next(2))
                down(0)
                down(1)
            ffn()

            def swap(side, t):
                begin_group()
                raw_group = t + 2 if t < 2 else 2 * t + 1
                pe.wait_ge(s_pr, before + raw_group + 1)
                for c in range(NCH):
                    last = matmul(PS[:, 3 * side + c, 0:CH], PERM, WK[:, 1 + t % 2, c * CH:(c + 1) * CH],
                                  start=True, stop=True)
                last.then_inc(s_mm, mm.up())
            before = pr.n
            dense(0, 0, wait_h=True)
            token_sums(next(ACCS))
            dense(1, 1, after=3, hook=broadcast)
            dense(0, 0)
            dense(1, 1)
            for t in range(KT):
                swap(0, t)
                dense(1, t % 2)
            swap(0, KT)
            swap(1, KT + 1)

            attention_pe(pe, transpose, PASSES)

            dense(0, 0, wait_h=True)
            dense(1, 1)
            with turns(pe, 1, KT // 2, {w: 2, started: 2, mm: 2, pr: 2}):
                dense(0, 0)
                dense(1, 1)
            ffn()

            token_sums(next(ACCS))
            pe.wait_ge(s_pr, pr.at())
            for m in range(KT):
                last = transpose(PS[0:HIST + NS, m // 4, (m % 4) * P:(m % 4 + 1) * P], CKEEP[:, m, :])
            last.then_inc(s_tr, tr.up())
            trr.n += 1
            for l in range(2):
                for part in range(2):
                    n = FT // 2
                    pe.wait_ge(s_trr, trr.at())
                    trr.n += 1
                    for f in range(n):
                        last = transpose(PS[0:2 + NS, 2 + f // 4, (f % 4) * P:(f % 4 + 1) * P],
                                         GKEEP[:, l, part * n + f, :])
                    last.then_inc(s_tr, tr.up())
            pe.wait_ge(s_trr, trr.at())
            pe.wait_ge(s_xg, KT)
            for b in range(NB):
                o = b % 2
                pe.wait_ge(s_trr, trr.at(1))
                trr.n += 1
                for m in range(KT):
                    last = transpose(PS[:, 2 * o + m // 4, (m % 4) * P:(m % 4 + 1) * P], X[:, m, b * P:(b + 1) * P])
                last.then_inc(s_tr, tr.up())
            pe.wait_ge(s_trr, trr.at(1))
            for m in range(KT):
                last = transpose(PS[0:NS, m // 4, (m % 4) * P:(m % 4 + 1) * P], X[:, m, SEQ:T])
            last.then_inc(s_tr, tr.up())


_INS = ["x_prompt", "x_sample", "state_conv", "cache_k", "cache_v", "state_ffn", "norm_mix", "norm_ffn", "norm_final",
        "conv_w_pw1", "conv_b_pw1", "conv_w_dw", "conv_b_dw", "conv_ln_g", "conv_ln_b", "conv_w_pw2", "conv_b_pw2",
        "attn_w_qkv", "attn_sinks", "attn_w_o", "ffn_w_in", "ffn_w_dw", "ffn_b_dw", "ffn_w_down"]
_OUTS = [("y_prompt", (1, SEQ, D)), ("y_sample", (NS, 1, D)),
         ("new_conv_prompt", (1, 1, HIST, D)), ("new_conv_sample", (1, NS, HIST, D)),
         ("new_k_prompt", (1, 1, WIN, NKV, HD)), ("new_v_prompt", (1, 1, WIN, NKV, HD)),
         ("new_k_sample", (1, NS, WIN, NKV, HD)), ("new_v_sample", (1, NS, WIN, NKV, HD)),
         ("new_ffn_prompt", (2, 1, 2, F)), ("new_ffn_sample", (2, NS, 2, F))]


def kernel(**inputs):
    import concourse.bacc as bacc
    from concourse.bass_utils import run_bass_kernel_spmd

    nc = bacc.Bacc("TRN2", target_bir_lowering=False, num_devices=1)
    arrays = {n: np.ascontiguousarray(inputs[n]) for n in _INS}
    arrays["const_small"], arrays["const_mask"], arrays["const_rope"] = constants()
    aps = {}
    for name, x in arrays.items():
        aps[name] = nc.dram_tensor(f"in_{name}", x.shape, F32, kind="ExternalInput").ap()
    for name, shape in _OUTS:
        aps[name] = nc.dram_tensor(f"out_{name}", shape, F32, kind="ExternalOutput").ap()
    build(nc, aps)
    r = run_bass_kernel_spmd(nc, [{f"in_{n}": x for n, x in arrays.items()}], core_ids=[0])
    return tuple(r.results[0][f"out_{name}"] for name, _ in _OUTS)
```

```python
from contextlib import ExitStack, contextmanager

import numpy as np

import concourse.bass as bass
from concourse import mybir

F32 = mybir.dt.float32
F32R = mybir.dt.float32r
ALU = mybir.AluOpType
ACT = mybir.ActivationFunctionType
AX = mybir.AxisListType.X

P = 128
D = 1024
KT = D // P
SEQ = 1024
NS = 8
T = SEQ + NS
NCH = 3
CH = T // NCH
BANK = 512
NB = SEQ // P
F = 2816
FT = F // P
CW = 31
HIST = CW - 1
NT = 11
NLATE = 3
NTA = 7
K_TILE = (6, 0)
HD = 64
GROUP = 4
NH = 16
NKV = 4
ROT = HD // 4
WIN = 128
EPS = 1e-6
SCALE = HD ** -0.5
MASKED = -1e30
PADK = P + T
WKC = HIST + T
WKP = -(-WKC // 8) * 8

R_MIX, R_FFN, R_FIN, R_B1, R_DW, R_BDW, R_LNG, R_LNB, R_B2 = 0, 2, 4, 5, 7, 38, 39, 40, 41
NPAR = 42
FR_W, FR_B, FR_ST, NFR = 0, 3, 4, 20

C_ID, C_ONE, C_PERM, C_SEL = 0, 128, 256, 384
NCONST = 392


def constants():
    ident = np.eye(P, dtype=np.float32)
    perm = np.zeros((P, P), np.float32)
    cos = np.ones((P, T), np.float32)
    sin = np.zeros((P, T), np.float32)
    half = ROT // 2
    theta = np.float32(500000.0)
    inv = (np.float32(1.0) / (theta ** (np.arange(0, ROT, 2, dtype=np.float32) / np.float32(ROT)))).astype(np.float32)
    pos = np.concatenate([np.arange(SEQ), np.full(NS, SEQ)]).astype(np.float32)
    ang = (inv[:, None] * pos[None, :]).astype(np.float32)
    for r in range(P):
        d = r % HD
        if d < ROT:
            perm[r - d + (d + half) % ROT, r] = 1.0
            cos[r] = np.cos(ang[d % half])
            sin[r] = np.sin(ang[d % half]) * np.float32(-1.0 if d < half else 1.0)
    sel = (np.arange(P)[:, None] // (P // NS) == np.arange(NS)[None, :]).astype(np.float32)
    small = np.concatenate([ident, np.ones((P, P), np.float32), perm, sel], axis=1)
    q, s = np.arange(P)[:, None], np.arange(2 * P)[None, :]
    band = (s >= q) & (s <= q + WIN)
    rest = np.where(band, np.float32(0), np.float32(MASKED))
    first = np.where(band & (s >= P), np.float32(0), np.float32(MASKED))
    mask = np.concatenate([first, first, rest, rest], axis=1).astype(np.float32)
    return small, mask, np.concatenate([cos, sin], axis=1)


class Count:

    def __init__(self):
        self.n, self.turn = 0, 0

    def up(self):
        self.n += 1
        return 1

    def next(self, by=1):
        self.n += by
        return self.at()

    def at(self, back=0):
        assert self.n - back > 0, "no wait is for less than one signal"
        return self.turn + (self.n - back)

    def due(self, back=0):
        return self.n - back > 0


@contextmanager
def turns(eng, first, last, counts):
    start = {c: c.n for c in counts}
    with eng.Fori(first, last) as i:
        for c, per in counts.items():
            c.turn = (i - first) * per if first else i * per
        yield i
        for c, per in counts.items():
            assert c.n - start[c] == per, (c.n - start[c], per)
    for c, per in counts.items():
        c.turn, c.n = 0, start[c] + per * (last - first)


def build(nc, a):
    ctx = ExitStack()
    with ctx:
        def sb(name, shape, dt=F32, stack=ctx):
            return stack.enter_context(nc.sbuf_tensor(name, shape, dt))

        def sem(name):
            return ctx.enter_context(nc.semaphore(name))

        X = sb("X", [P, KT, T])
        W = sb("W", [P, 2, 2, D], F32R)
        RAW = sb("RAW", [P, 2, D])
        CST = sb("CST", [P, NCONST])
        PAR = sb("PAR", [P, KT, NPAR])
        FPAR = sb("FPAR", [P, FT, 2 * NFR])
        TOK = sb("TOK", [P, 4, NB + 1])
        CKEEP = sb("CKEEP", [P, KT, HIST + NS])
        NSINK = sb("NSINK", [P, NH])
        SINKC = sb("SINKC", [NH, 2])
        EPSC = sb("EPSC", [P, 1])
        SMALL = sb("SMALL", [P, 2, 7, GROUP])
        with ExitStack() as s:
            sb("skip_tiles_0_1", [P, 2, WKP], F32, s)
            GSPLIT = sb("GSPLIT", [P, 2, WKP], F32R, s)
            sb("skip_tile_4", [P, WKP], F32, s)
            DIAGB = sb("DIAGB", [P, 2, NT - NTA, P], F32R, s)
            sb("skip_tiles_6_8", [P, 4 * WKP - 2 * (NT - NTA) * P], F32, s)
            DIAGA = sb("DIAGA", [P, 2, NTA, P], F32R, s)
        WK = sb("WK", [P, 9, WKP])
        GKEEP = sb("GKEEP", [P, 2, FT, 2 + NS])
        PBLK = sb("PBLK", [P, NS, NS, NH])
        TAPLO = WK[:, 6, 256:256 + KT * NT].rearrange("p (m k) -> p m k", m=KT)
        TAPHI = GSPLIT[:, 0, 0:KT * NT].rearrange("p (m k) -> p m k", m=KT)
        sb("diagonals_end", [P, max(0, 2 * NTA * P - 2 * FT * (2 + NS) - NS * NS * NH)])
        with ExitStack() as s:
            XIN = sb("XIN", [P, NB, D], F32, s)
        with ExitStack() as s:
            CONV = sb("CONV", [P, KT, T], F32, s)
        with ExitStack() as s:
            MID = sb("MID", [P, 2, 2, T], F32R, s)
        with ExitStack() as s:
            YOUT = sb("YOUT", [P, NB, D], F32, s)
        QA = sb("QA", [P, 2, GROUP, T])
        with ExitStack() as s:
            H = sb("H", [P, 2, KT, T], F32R, s)
        KR = sb("KR", [P, 2, 2, PADK], F32R)
        VR = sb("VR", [P, 2, NB + 1, NKV * HD], F32R)
        MASK = sb("MASK", [P, 2, BANK], F32R)
        QS = sb("QS", [P, 2, 2, BANK], F32R)
        PX = sb("PX", [P, 2, GROUP, 2 * P])
        PT = sb("PT", [P, 2, 2, BANK], F32R)
        IDR = sb("IDR", [P, P], F32R)
        PS = ctx.enter_context(nc.psum_tensor("PS", [P, 8, BANK], F32))

        IDENT, ONES, PERM = (CST[:, c:c + P] for c in (C_ID, C_ONE, C_PERM))
        SEL = CST[:, C_SEL:C_SEL + NS]
        RS, ACC = WK[:, 0, 0:T], WK[:, 1, 0:T]
        SQ = [WK[:, 2, 0:T], WK[:, 3, 0:T]]
        COS, SIN = WK[:, 7, 0:T], WK[:, 8, 0:T]
        HISTORY = WK[:, 7:9, :].rearrange("p a n -> p (a n)")[:, 0:KT * NS * HIST]

        def chunks(ap):
            return ap.rearrange("p (c n) -> p c n", c=NCH)

        def par(m, r):
            if isinstance(m, int):
                return PAR[:, m, r:r + 1]
            return PAR[:, bass.ds(m, 1), r:r + 1].rearrange("p a b -> p (a b)")

        def fpar(f, r, n=1):
            if isinstance(f, int):
                return FPAR[:, f, r:r + n]
            return FPAR[:, bass.ds(f, 1), r:r + n].rearrange("p a b -> p (a b)")

        def tile(t, m, lo=0, hi=T):
            if isinstance(m, int):
                return t[:, m, lo:hi]
            return t[:, bass.ds(m, 1), lo:hi].rearrange("p a b -> p (a b)")

        def htile(part, m):
            if isinstance(m, int):
                return H[:, part, m, :]
            return H[:, part, bass.ds(m, 1), :].rearrange("p a b -> p (a b)")

        s_const = sem("const_loaded")
        s_rows = sem("rows_loaded")
        s_x = sem("x_loaded")
        s_tab = sem("tables_loaded")
        s_cache = sem("cache_loaded")
        s_raw = [sem("raw_loaded0"), sem("raw_loaded1")]
        s_hi = sem("weight_hi")
        s_go = sem("split_may_start")
        s_w = sem("weight_ready")
        s_wstart = sem("weight_started")
        s_tr = sem("transposed")
        s_trr = sem("transpose_taken")
        s_mm = sem("dense_done")
        s_pr = sem("dense_taken")
        s_sq = sem("square_ready")
        s_acc = sem("accumulated")
        s_hh = sem("h_hi_ready")
        s_h = sem("h_ready")
        s_sum = sem("sums_done")
        s_root = sem("roots_ready")
        s_rec = sem("token_scale_ready")
        s_bc = sem("broadcast_done")
        s_bcr = sem("broadcast_taken")
        s_sqd = sem("square_summed")
        s_v = sem("dve_own")
        s_sig = sem("sigmoid_ready")
        s_glu = sem("glu_ready")
        s_tap0 = sem("first_tap")
        s_taplo = sem("tap_weights_lo")
        s_taphi = sem("tap_weights_hi")
        s_gh = sem("glu_hi")
        s_gs = sem("glu_split")
        s_diag = sem("tap_diagonals_ready")
        s_td = sem("last_taps_done")
        s_cs = sem("conv_summed")
        s_rs = sem("layer_norm_scale_ready")
        s_cg = sem("upper_tiles_normed")
        s_tt = sem("last_taps_taken")
        s_conv = sem("conv_done")
        s_t2 = sem("last_tap")
        s_gc = sem("gate_conv")
        s_silu = sem("silu_ready")
        s_m = sem("mid_ready")
        s_mh = sem("mid_hi")
        s_mid = sem("mid_split")
        s_heads = sem("heads_ready")
        s_kvh = sem("kv_hi")
        s_kv = sem("kv_ready")
        s_kvo = sem("kv_turned")
        s_kvr = sem("kv_rows_taken")
        s_qh = sem("q_hi")
        s_qs = sem("q_split")
        s_sc = sem("scores_done")
        s_nm = sem("negative_max")
        s_ex = sem("exp_done")
        s_pd = sem("inverse_sums_ready")
        s_pn = sem("probs_ready")
        s_pt = sem("probs_turned")
        s_pth = sem("probs_hi")
        s_ptl = sem("probs_split")
        s_pv = sem("heads_done")
        s_ov = sem("heads_taken")
        s_small = sem("small_values")
        s_svx = sem("sample_scores_shifted")
        s_sm = sem("sample_mm")
        s_sv = sem("sample_dve")
        s_sa = sem("sample_act")
        s_xg = sem("x_gained")
        s_ka = sem("gate_rows_taken_by_act")
        s_ya = sem("odd_y_blocks_taken")
        s_st = sem("stores")

        up = "(k p) n -> p k n"
        w_pw1 = a["conv_w_pw1"][0].rearrange(up, p=P)
        w_pw2 = a["conv_w_pw2"][0].rearrange(up, p=P)
        w_qkv = a["attn_w_qkv"][0].rearrange(up, p=P)
        w_in = [a["ffn_w_in"][l].rearrange(up, p=P) for l in range(2)]
        w_dn = [a["ffn_w_down"][l].rearrange("(t p) n -> p t n", p=P) for l in range(2)]
        w_o = a["attn_w_o"][0].rearrange("(a h g d) n -> h d a g n", a=2, h=2, g=GROUP)

        acc_marks = []
        GROWS = [WK[:, 6:9, :].rearrange("p a n -> p (a n)"), WK[:, 0:3, :].rearrange("p a n -> p (a n)")]
        HALF_F = F // 2

        def GATE_PS(part):
            return PS[0:2 + NS, 2 + 3 * part:5 + 3 * part, :].rearrange("p a n -> p (a n)")[:, 0:HALF_F]

        def Y_PS(b):
            pair = 2 * (b % 4)
            return PS[:, pair:pair + 2, :].rearrange("p a n -> p (a n)")
        LNSQ = [WK[:, 2, 0:T], WK[:, 5, 0:T]]
        LNOUT = LNSQ + [WK[:, 4, 0:T]]
        UNITS = [(n, p, hf) for n in range(NB) for p in range(2) for hf in range(2)]
        HEADS, KV_READY = 2 + 2 * KT, 5
        ROW_DMAS = 20
        STORES = 23
        block = ctx.enter_context(nc.Block())

        @block.sync
        def _(sp):
            ready = Count()
            n = [0]

            def load(src_halves, slot):
                if n[0] >= 2:
                    sp.wait_ge(s_w, ready.at(1))
                n[0] += 1
                for h, src in enumerate(src_halves):
                    dst = RAW[h * HD:(h + 1) * HD, slot, :]
                    dst = dst.rearrange("p (k n) -> p k n", k=src.shape[-2])
                    sp.dma_start(dst, src).then_inc(s_raw[slot], 16)
                ready.n += 1

            def halves(w, col):
                return [w[h * HD:(h + 1) * HD, :, bass.ds(col, P)] for h in range(2)]

            def down(l, i, half):
                return [w_dn[l][h * HD:(h + 1) * HD, bass.ds(i * 2, 2), half * BANK:(half + 1) * BANK]
                        for h in range(2)]

            def ffn(l):
                def gate(f, slot):
                    load(halves(w_in[l], f * P), slot)

                def upp(f, slot):
                    load(halves(w_in[l], f * P + F), slot)
                gate(0, 0)
                upp(0, 1)
                gate(1, 0)
                upp(1, 1)
                with turns(sp, 1, FT // 2, {ready: 6}) as i:
                    gate(i * 2, 0)
                    load(down(l, i - 1, 0), 1)
                    load(down(l, i - 1, 1), 0)
                    upp(i * 2, 1)
                    gate(i * 2 + 1, 0)
                    upp(i * 2 + 1, 1)
                load(down(l, FT // 2 - 1, 0), 0)
                load(down(l, FT // 2 - 1, 1), 1)

            load(halves(w_pw1, 0), 0)
            load(halves(w_pw1, D), 1)
            with turns(sp, 1, KT, {ready: 2}) as i:
                load(halves(w_pw1, i * P), 0)
                load(halves(w_pw1, i * P + D), 1)
            with turns(sp, 0, KT // 2, {ready: 2}) as i:
                load(halves(w_pw2, i * 2 * P), 0)
                load(halves(w_pw2, i * 2 * P + P), 1)
            ffn(0)
            vcol, kcol = (NH + NKV) * HD, NH * HD
            for j, col in enumerate([vcol, vcol + P, kcol, kcol + P]):
                load(halves(w_qkv, col), j % 2)
            with turns(sp, 0, KT // 2, {ready: 2}) as i:
                load(halves(w_qkv, i * 2 * P), 0)
                load(halves(w_qkv, i * 2 * P + P), 1)

            sp.wait_ge(s_kv, KV_READY)
            kn, vn = a["new_k_prompt"], a["new_v_prompt"]
            sp.dma_start(kn[0, 0].rearrange("w j d -> w (j d)"), WK[:, 8, BANK:BANK + 256]).then_inc(s_st, 16)
            sp.dma_start(vn[0, 0].rearrange("w j d -> w (j d)"), WK[:, 8, BANK + 256:2 * BANK]).then_inc(s_st, 16)
            for c, new in ((0, "new_v_sample"), (256, "new_k_sample")):
                sp.dma_start(a[new][0, :, WIN - 1].rearrange("b j d -> b (j d)"), WK[0:NS, 8, c:c + 256]).then_inc(s_st, 16)
            for c, old in ((0, "cache_k"), (2, "cache_v")):
                src = a[old][0].rearrange("b (q w) j d -> (b q) (w j d)", q=16)
                sp.dma_start(WK[:, c:c + 2, 0:D], src.rearrange("p (a n) -> p a n", a=2)).then_inc(s_cache, 16)

            def wo(m, slot):
                sp.wait_ge(s_w, ready.at(1))
                for h in range(2):
                    for b in range(2):
                        dst = RAW[h * HD:(h + 1) * HD, slot, b * BANK:(b + 1) * BANK]
                        sp.dma_start(dst.rearrange("p (g n) -> p g n", g=GROUP),
                                     w_o[h, :, b, :, bass.ds(m * P, P)]).then_inc(s_raw[slot], 8 * 2)
                ready.n += 1
            with turns(sp, 0, KT // 2, {ready: 2}) as i:
                wo(i * 2, 0)
                wo(i * 2 + 1, 1)
            ffn(1)
            yr = Count()
            yr.n = 2 + KT + 3
            for n_ in range(NB):
                if n_ % 2 == 0:
                    sp.wait_ge(s_trr, yr.next())
                else:
                    sp.wait_ge(s_ya, n_ // 2 + 1)
                sp.dma_start(a["y_prompt"][0, n_ * P:(n_ + 1) * P, :], YOUT[:, n_, :]).then_inc(s_st, 16)
            sp.wait_ge(s_trr, yr.next())
            sp.dma_start(a["y_sample"][:, 0, :], WK[0:NS, 4, 0:D]).then_inc(s_st, 16)
            sp.wait_ge(s_st, 16 * STORES)

        @block.gpsimd
        def _(pool):
            started, ready, hi = Count(), Count(), Count()
            raw = [Count(), Count()]

            def split(slot, per, free):
                pool.wait_ge(s_raw[slot], raw[slot].next(per))
                if free:
                    pool.wait_ge(s_wstart, started.at())
                started.n += 1
                pool.sem_inc(s_go, 1)
                nc.gpsimd.tensor_copy(W[:, slot, 0, :], RAW[:, slot, :]).then_inc(s_hi, hi.up())
                pool.wait_ge(s_hi, hi.at())
                nc.gpsimd.tensor_tensor(W[:, slot, 1, :], RAW[:, slot, :],
                                                  W[:, slot, 0, :].bitcast(F32), ALU.subtract).then_inc(s_w, ready.up())

            def stretch(count, per=32):
                with turns(pool, 0, count // 2, {started: 2, ready: 2, hi: 2, raw[0]: per, raw[1]: per}):
                    split(0, per, True)
                    split(1, per, True)

            split(0, 32, False)
            split(1, 32, True)
            n_ffn = 3 * FT
            tt, cg = Count(), Count()

            def add_conv(i):
                pool.wait_ge(s_tt, tt.next())
                if tt.n > 1:
                    pool.wait_ge(s_cs, tt.at(1))
                nc.gpsimd.tensor_tensor(ACC, ACC, tile(CONV, i), ALU.add).then_inc(s_cs, 1)
            split(0, 32, True)
            split(1, 32, True)
            split(0, 32, True)
            split(1, 32, True)
            add_conv(0)
            with turns(pool, 3, KT, {started: 2, ready: 2, hi: 2, raw[0]: 32, raw[1]: 32, tt: 1}) as i:
                split(0, 32, True)
                split(1, 32, True)
                add_conv(i - 2)
            split(0, 32, True)
            add_conv(KT - 2)
            add_conv(KT - 1)
            pool.wait_ge(s_rs, 1)
            for m in range(KT // 2, KT):
                nc.gpsimd.tensor_tensor(CONV[:, m, :], CONV[:, m, :], RS, ALU.mult).then_inc(s_cg, 1)
            split(1, 32, True)
            stretch(KT - 2 + n_ffn + 4 + KT)
            for u, (n, p, hf) in enumerate(UNITS):
                pool.wait_ge(s_pd, u + 1)
                nc.gpsimd.tensor_tensor(PX[:, hf], PX[:, hf],
                                        SMALL[:, hf, 6, :].unsqueeze(2).broadcast_to((P, GROUP, 2 * P)),
                                        ALU.mult).then_inc(s_pn, 1)
            split(0, 64, True)
            split(1, 64, True)
            stretch(KT - 2, 64)
            stretch(n_ffn)

        def attention_dve(dve):
            v = nc.vector
            own = Count()
            kvh, qh, qs = Count(), Count(), Count()
            sc, nm, ex, pn = Count(), Count(), Count(), Count()
            pth, ptl = Count(), Count()
            sv = Count()
            small = Count()

            v.memset(KR[:, :, :, 0:P].bitcast(F32), 0.0).then_inc(s_kv, own.up())
            v.memset(VR[:, :, 0, :].bitcast(F32), 0.0).then_inc(s_kv, own.up())
            dve.wait_ge(s_kvo, 1)
            v.tensor_copy(WK[0:NS, 8, 0:BANK], PS[0:NS, 4, :])
            v.tensor_copy(WK[:, 8, BANK:BANK + 256], PS[:, 5, 0:256])
            v.tensor_copy(WK[:, 8, BANK + 256:2 * BANK], PS[:, 3, 256:BANK]).then_inc(s_kvr, 1)
            for p in range(2):
                dve.wait_ge(s_kvh, kvh.next())
                v.tensor_tensor(KR[:, 1, p, P:PADK], WK[:, K_TILE[p], 0:T], KR[:, 0, p, P:PADK].bitcast(F32),
                                        ALU.subtract).then_inc(s_kv, own.up())
            dve.wait_ge(s_kvh, kvh.next(2))
            v.tensor_tensor(VR[:, 1, 1:NB + 1, :].rearrange("p (a b) n -> p a (b n)", b=2), PS[:, 0:4, :],
                                    VR[:, 0, 1:NB + 1, :].rearrange("p (a b) n -> p a (b n)", b=2).bitcast(F32),
                                    ALU.subtract).then_inc(s_kv, own.up())
            assert own.n == KV_READY

            def q_lo(n, p):
                dve.wait_ge(s_qh, qh.next())
                v.tensor_tensor(QS[:, p, 1, :].rearrange("p (g n) -> p g n", g=GROUP),
                                       QA[:, p, :, n * P:(n + 1) * P],
                                       QS[:, p, 0, :].rearrange("p (g n) -> p g n", g=GROUP).bitcast(F32), ALU.subtract).then_inc(s_qs, qs.up())

            def stats(n, p, hf):
                j = 2 * p + hf
                dve.wait_ge(s_sc, sc.next())
                v.tensor_reduce(SMALL[:, hf, 0, :],
                                            PS[:, 2 * hf:2 * hf + 2, :].rearrange("p a (g n) -> p (a g) n", g=2), AX, ALU.max).then_inc(s_small, small.up())
                dve.wait_ge(s_small, small.at())
                nsink = NSINK[:, j * GROUP:(j + 1) * GROUP]
                v.scalar_tensor_tensor(SMALL[:, hf, 1, :], SMALL[:, hf, 0, :], -SCALE, nsink, ALU.mult, ALU.min).then_inc(s_nm, nm.up())
                dve.wait_ge(s_nm, nm.at())
                v.tensor_tensor(SMALL[:, hf, 2, :], SMALL[:, hf, 1, :], nsink, ALU.subtract).then_inc(s_nm, nm.up())

            def norm(n, p, hf):
                dve.wait_ge(s_ex, ex.next())
                v.tensor_tensor(SMALL[:, hf, 5, :], SMALL[:, hf, 3, :], SMALL[:, hf, 4, :], ALU.add).then_inc(s_small, small.up())
                dve.wait_ge(s_small, small.at())
                v.reciprocal(SMALL[:, hf, 6, :], SMALL[:, hf, 5, :]).then_inc(s_pd, pn.up())

            def probs_lo():
                dve.wait_ge(s_pth, pth.next())
                v.tensor_tensor(PT[:, 1], PS[:, 4:6, :], PT[:, 0].bitcast(F32), ALU.subtract).then_inc(s_ptl, ptl.up())

            q_lo(0, 0)
            stats(*UNITS[0])
            q_lo(0, 1)
            stats(*UNITS[1])
            norm(*UNITS[0])
            for u in range(len(UNITS)):
                if u + 2 < len(UNITS):
                    stats(*UNITS[u + 2])
                if u + 1 < len(UNITS):
                    norm(*UNITS[u + 1])
                probs_lo()
                if u + 4 < len(UNITS) and UNITS[u + 4][2] == 0:
                    q_lo(*UNITS[u + 4][:2])

            smm, sa = Count(), Count()
            Z = WK[:, 6, :]
            qb = Z[:, 0:256].rearrange("p (a b h) -> p a b h", a=2, b=NS)
            dve.wait_ge(s_sm, smm.next())
            v.tensor_copy(WK[:, 4:6, 0:D], PS[:, 0:4, :].rearrange("p (a b) n -> p a (b n)", b=2)).then_inc(s_sv, sv.up())
            v.memset(Z[:, 0:256], 0.0).then_inc(s_small, small.up())
            dve.wait_ge(s_small, small.at())
            for p in range(2):
                for hf in range(2):
                    rows, h0 = slice(hf * HD, (hf + 1) * HD), (2 * p + hf) * GROUP
                    last = v.tensor_copy(qb[rows, p, :, h0:h0 + GROUP].rearrange("p b g -> p g b"), QA[rows, p, :, SEQ:T])
            last.then_inc(s_sv, sv.up())
            dve.wait_ge(s_sm, smm.next())
            ss, sn = WK[0:NH, 7, 0:D], WK[0:NH, 7, D:D + NS]
            sw = ss.rearrange("p (w b q) -> p w b q", w=8, b=NS)
            sbw = ss.rearrange("p (w b q) -> p b w q", w=8, b=NS)
            mx, neg, es, den = (Z[0:NH, c:c + NS] for c in (384, 392, 400, 408))

            def wide(x):
                return x.unsqueeze(1).unsqueeze(3).broadcast_to((NH, 8, NS, 16))
            for b in range(NS):
                v.tensor_scalar(sw[:, :, b, :], PS[0:NH, 4 + b // 4, (b % 4) * P:(b % 4 + 1) * P].rearrange("p (w q) -> p w q", w=8),
                                SCALE, None, ALU.mult)
            v.tensor_scalar(sn, PS[0:NH, 6, 0:NS], SCALE, None, ALU.mult).then_inc(s_small, small.up())
            dve.wait_ge(s_small, small.at())
            v.tensor_reduce(mx, sbw, mybir.AxisListType.XY, ALU.max).then_inc(s_small, small.up())
            dve.wait_ge(s_small, small.at())
            v.tensor_tensor(mx, mx, sn, ALU.max).then_inc(s_small, small.up())
            dve.wait_ge(s_small, small.at())
            v.tensor_scalar(neg, mx, -1.0, SINKC[:, 1:2], ALU.mult, ALU.min).then_inc(s_small, small.up())
            dve.wait_ge(s_small, small.at())
            svx = Count()
            v.tensor_tensor(sn, sn, neg, ALU.add).then_inc(s_small, small.up())
            dve.wait_ge(s_small, small.at())
            v.tensor_tensor(sw, sw, wide(neg), ALU.add).then_inc(s_svx, svx.up())
            dve.wait_ge(s_sa, sa.next())
            v.tensor_reduce(den, sbw, mybir.AxisListType.XY, ALU.add).then_inc(s_small, small.up())
            dve.wait_ge(s_small, small.at())
            v.tensor_tensor(den, den, es, ALU.add).then_inc(s_small, small.up())
            dve.wait_ge(s_small, small.at())
            v.tensor_tensor(den, den, sn, ALU.add).then_inc(s_small, small.up())
            dve.wait_ge(s_small, small.at())
            v.reciprocal(mx, den).then_inc(s_small, small.up())
            dve.wait_ge(s_small, small.at())
            v.tensor_tensor(sn, sn, mx, ALU.mult).then_inc(s_small, small.up())
            dve.wait_ge(s_small, small.at())
            v.tensor_tensor(sw, sw, wide(mx), ALU.mult).then_inc(s_sv, sv.up())
            dve.wait_ge(s_sm, smm.next())
            v.tensor_copy(Z[:, 416:416 + P], PS[:, 0, 0:P]).then_inc(s_small, small.up())
            dve.wait_ge(s_small, small.at())
            v.tensor_copy(Z[0:NS, 544:544 + NH], PS[0:NS, 0, P:P + NH]).then_inc(s_small, small.up())
            dve.wait_ge(s_small, small.at())
            pts = Z[:, 416:416 + P].rearrange("p (w h) -> p w h", w=8)
            for k in range(8):
                v.tensor_tensor(PBLK[:, k], pts[:, k, :].unsqueeze(1).broadcast_to((P, NS, NH)),
                                SEL.unsqueeze(2).broadcast_to((P, NS, NH)), ALU.mult)
            v.tensor_tensor(Z[0:NS, 256:256 + P].rearrange("p (b h) -> p b h", b=NS),
                                   Z[0:NS, 544:544 + NH].unsqueeze(1).broadcast_to((NS, NS, NH)),
                                   IDENT[0:NS, 0:NS].unsqueeze(2).broadcast_to((NS, NS, NH)), ALU.mult).then_inc(s_sv, sv.up())
            dve.wait_ge(s_sm, smm.next())
            for p in range(2):
                for hf in range(2):
                    rows, h0 = slice(hf * HD, (hf + 1) * HD), (2 * p + hf) * GROUP
                    src = PS[rows, 1, p * P:(p + 1) * P].rearrange("p (b h) -> p h b", b=NS)[:, h0:h0 + GROUP, :]
                    last = v.tensor_copy(QA[rows, p, :, SEQ:T], src)
            last.then_inc(s_sv, sv.up())
            dve.wait_ge(s_sv, sv.at())

        @block.vector
        def _(dve):
            own = Count()
            tr, trr = Count(), Count()
            mm, pr = Count(), Count()
            sq, acc = Count(), Count()
            hh, h = Count(), Count()
            sums, root, rec, bc, bcr = (Count() for _ in range(5))
            v = nc.vector

            def side(s):
                return PS[:, 3 * s:3 * s + 3, 0:CH]

            def split_lo(m, x, gain=None):
                dve.wait_ge(s_hh, hh.next())
                if gain is None:
                    v.tensor_tensor(htile(1, m), x, htile(0, m).bitcast(F32), ALU.subtract).then_inc(s_h, h.up())
                else:
                    v.scalar_tensor_tensor(htile(1, m), x, gain, htile(0, m).bitcast(F32),
                                                 ALU.mult, ALU.subtract).then_inc(s_h, h.up())

            def add_square(o):
                dve.wait_ge(s_sq, sq.next())
                dve.wait_ge(s_acc, acc.at())
                v.tensor_tensor(ACC, ACC, SQ[o], ALU.add).then_inc(s_acc, acc.up())

            def clear_acc():
                if sums.due():
                    dve.wait_ge(s_sum, sums.at())
                v.memset(ACC, 0.0).then_inc(s_acc, acc.up())

            def token_scale():
                dve.wait_ge(s_root, root.next())
                v.reciprocal(TOK[:, 2, :], TOK[:, 1, :]).then_inc(s_rec, rec.up())

            def norm_scale():
                sums.n += 1
                token_scale()
                dve.wait_ge(s_bc, bc.next())
                v.tensor_copy(RS[:, 0:SEQ].rearrange("p (c n) -> p c n", c=2), PS[:, 6:8, :]).then_inc(s_bcr, bcr.up())
                dve.wait_ge(s_bc, bc.next())
                v.tensor_copy(RS[:, SEQ:T], PS[:, 6, 0:NS]).then_inc(s_bcr, bcr.up())
                dve.wait_ge(s_bcr, bcr.at())

            def x_add(m, s, bias=None):
                dve.wait_ge(s_mm, mm.next())
                x = chunks(tile(X, m))
                if bias is None:
                    v.tensor_tensor(x, side(s), x, ALU.add).then_inc(s_pr, pr.up())
                else:
                    v.scalar_tensor_tensor(x, side(s), bias, x, ALU.add, ALU.add).then_inc(s_pr, pr.up())

            def residual(side_of, bias, wide, row):
                clear_acc()

                def one(m):
                    x_add(m, side_of(m % 2), None if bias is None else par(m, bias))
                with turns(dve, 0, KT // 2 - 1, {mm: 2, pr: 2, sq: 2, acc: 2}) as i:
                    for o in range(2):
                        x_add(i * 2 + o, side_of(o), None if bias is None else par(i * 2 + o, bias))
                        if not wide:
                            add_square(o)
                    if wide:
                        add_square(0)
                        add_square(1)
                one(KT - 2)
                if not wide:
                    add_square(0)
                one(KT - 1)
                if row is not None:
                    for m in range(2):
                        split_lo(m, X[:, m, :], par(m, row))
                if wide:
                    add_square(0)
                add_square(1)
                acc_marks.append(acc.n)
                if row is not None:
                    with turns(dve, 2, KT, {hh: 1, h: 1}) as m:
                        split_lo(m, tile(X, m), par(m, row))

            v.memset(EPSC[:, :], EPS)
            v.memset(TOK[:, :, :], 1.0).then_inc(s_v, own.up())
            dve.wait_ge(s_v, own.at())
            dve.wait_ge(s_tr, tr.next())
            v.tensor_copy(FPAR[:, 0:12, :].rearrange("p m r -> p (m r)"), PS[:, 5, 0:12 * 2 * NFR])
            v.tensor_copy(FPAR[:, 12:FT, :].rearrange("p m r -> p (m r)"), PS[:, 6, 0:10 * 2 * NFR])
            v.tensor_copy(X[:, :, SEQ:T], PS[:, 7, 0:KT * NS].rearrange("p (m n) -> p m n", m=KT))
            v.tensor_scalar(NSINK[:, :], PS[:, 7, 64:64 + NH], -1.0, None, ALU.mult).then_inc(s_acc, acc.up())
            v.tensor_scalar(SINKC[:, 1:2], SINKC[:, 0:1], -1.0, None, ALU.mult)
            v.tensor_copy(PAR[:, :, :].rearrange("p m r -> p (m r)"), PS[:, 0, 0:KT * NPAR]).then_inc(s_trr, trr.up())
            v.tensor_copy(HISTORY.rearrange("p (a n) -> p a n", a=4), PS[:, 1:5, 0:2 * NS * HIST]).then_inc(s_trr, trr.up())
            clear_acc()
            with turns(dve, 0, KT // 2, {tr: 2, trr: 2, hh: 2, h: 2}) as i:
                for o in range(2):
                    dve.wait_ge(s_tr, tr.next())
                    x = X[:, bass.ds(i * 2 + o, 1), 0:SEQ].rearrange("p a (c n) -> p (a c) n", c=2)
                    v.tensor_copy(x, PS[:, 2 * o:2 * o + 2, :]).then_inc(s_trr, trr.up())
                for o in range(2):
                    split_lo(i * 2 + o, tile(X, i * 2 + o), par(i * 2 + o, R_MIX))
            with turns(dve, 0, KT // 2, {sq: 2, acc: 2}):
                for o in range(2):
                    add_square(o)
            acc_marks.append(acc.n)

            norm_scale()
            sig, glu, tap0, gh, gs, td, tt = (Count() for _ in range(7))
            GL, TA, TG, SIG, TM = (WK[:, k, :] for k in (4, 2, 3, 5, 6))
            sig.n = tap0.n = 1
            dve.wait_ge(s_taphi, 1)
            v.tensor_tensor(TAPLO, PAR[:, :, R_DW + CW - NT:R_DW + CW], TAPHI.bitcast(F32),
                            ALU.subtract).then_inc(s_taplo, 1)
            v.memset(GL[:, 0:HIST], 0.0).then_inc(s_v, own.up())
            dve.wait_ge(s_v, own.at())
            clear_acc()

            def scale_tile():
                dve.wait_ge(s_mm, mm.next())
                dve.wait_ge(s_v, own.at())
                v.tensor_tensor(chunks(TA[:, 0:T]), side(0), chunks(RS), ALU.mult).then_inc(s_pr, pr.up())
                dve.wait_ge(s_mm, mm.next())
                dve.wait_ge(s_sig, sig.at())
                v.tensor_tensor(chunks(TG[:, 0:T]), side(1), chunks(RS), ALU.mult).then_inc(s_pr, pr.up())

            def conv_taps(i, lo, hi):
                c = tile(CONV, i, 0, SEQ)
                for k in range(lo, hi):
                    v.scalar_tensor_tensor(c, GL[:, k:k + SEQ], par(i, R_DW + k), c, ALU.mult, ALU.add).then_inc(s_v, own.up())
                    dve.wait_ge(s_v, own.at())

            def finish_tile(i):
                conv_taps(i, CW - NT - NLATE, CW - NT)
                if isinstance(i, int):
                    c2 = CONV[:, i, 0:SEQ].rearrange("p (c n) -> p c n", c=2)
                else:
                    c2 = CONV[:, bass.ds(i, 1), 0:SEQ].rearrange("p a (c n) -> p (a c) n", c=2)
                v.tensor_tensor(c2, PS[:, 6:8, :], c2, ALU.add).then_inc(s_tt, tt.up())

            def conv_tile(i):
                dve.wait_ge(s_sig, sig.next())
                dve.wait_ge(s_tap0, tap0.at())
                v.scalar_tensor_tensor(GL[:, HIST:WKC], TA[:, 0:T], par(i, R_B1), SIG[:, 0:T], ALU.add, ALU.mult).then_inc(s_glu, glu.up())
                n = NS * HIST
                hist = HISTORY[:, i * n:(i + 1) * n] if isinstance(i, int) else HISTORY[:, bass.ds(i * n, n)]
                taps = par_taps(i)
                v.tensor_tensor(TM[:, 0:240].rearrange("p (b k) -> p b k", b=NS),
                                     hist.rearrange("p (b k) -> p b k", b=NS),
                                     taps.unsqueeze(1).broadcast_to((P, NS, HIST)), ALU.mult).then_inc(s_v, own.up())
                dve.wait_ge(s_v, own.at())
                v.tensor_reduce(TM[:, 240:248], TM[:, 0:240].rearrange("p (b k) -> p b k", b=NS), AX, ALU.add).then_inc(s_v, own.up())
                dve.wait_ge(s_v, own.at())
                dve.wait_ge(s_glu, glu.at())
                v.scalar_tensor_tensor(TM[:, 248:256], GL[:, HIST + SEQ:WKC], par(i, R_DW + HIST), TM[:, 240:248],
                                            ALU.mult, ALU.add).then_inc(s_v, own.up())
                dve.wait_ge(s_v, own.at())
                dve.wait_ge(s_gh, gh.next())
                v.tensor_tensor(GSPLIT[:, 1, 0:WKC], GL[:, 0:WKC], GSPLIT[:, 0, 0:WKC].bitcast(F32), ALU.subtract).then_inc(s_gs, gs.up())
                dve.wait_ge(s_tap0, tap0.next())
                v.tensor_scalar(tile(CONV, i, SEQ, T), TM[:, 248:256], par(i, R_BDW), None, ALU.add).then_inc(s_v, own.up())
                conv_taps(i, 1, CW - NT - NLATE)

            def par_taps(i):
                if isinstance(i, int):
                    return PAR[:, i, R_DW:R_DW + HIST]
                return PAR[:, bass.ds(i, 1), R_DW:R_DW + HIST].rearrange("p a b -> p (a b)")

            scale_tile()
            with turns(dve, 0, KT - 1, {mm: 2, pr: 2, sig: 1, glu: 1, own: 4 + CW - 1 - NT, tap0: 1,
                                        gh: 1, gs: 1, td: 1, tt: 1}) as i:
                conv_tile(i)
                dve.wait_ge(s_td, td.next())
                scale_tile()
                finish_tile(i)
            conv_tile(KT - 1)
            dve.wait_ge(s_td, td.next())
            finish_tile(KT - 1)
            MU = TG[:, 0:T]
            dve.wait_ge(s_sum, sums.next())
            v.tensor_scalar(chunks(MU), side(0), 1.0 / D, None, ALU.mult).then_inc(s_v, own.up())
            dve.wait_ge(s_v, own.at())
            cen = Count()
            with turns(dve, 0, KT, {cen: 1}) as i:
                c = tile(CONV, i)
                v.tensor_tensor(c, c, MU, ALU.subtract).then_inc(s_conv, cen.up())
            sq.n += KT
            dve.wait_ge(s_root, root.next())
            v.reciprocal(RS, RS).then_inc(s_rs, 1)
            dve.wait_ge(s_rs, 1)

            def normed(m):
                v.tensor_tensor(CONV[:, m, :], CONV[:, m, :], RS, ALU.mult).then_inc(s_conv, cen.up())
            for m in range(2):
                normed(m)
            for m in range(KT):
                if m + 2 < KT // 2:
                    normed(m + 2)
                dve.wait_ge(s_hh, hh.next())
                v.tensor_tensor(H[:, 1, m, :], LNOUT[m % 3], H[:, 0, m, :].bitcast(F32), ALU.subtract).then_inc(s_h, h.up())
            residual(lambda o: o, R_B2, False, R_FFN)

            t2, gc, silu, m_, mh, mid = (Count() for _ in range(6))
            silu.n = KT
            GB, TT, MM = WK[:, 4, :], WK[:, 5, 0:T], WK[:, 6, 0:T]

            def ffn(l):
                norm_scale()
                base = l * NFR
                v.memset(GB[:, 0:2], 0.0).then_inc(s_v, own.up())
                dve.wait_ge(s_v, own.at())

                def gate(s, f, adds=()):
                    dve.wait_ge(s_mm, mm.next())
                    if t2.due():
                        dve.wait_ge(s_t2, t2.at())
                    v.tensor_tensor(chunks(GB[:, 2:2 + T]), side(s), chunks(RS), ALU.mult).then_inc(s_pr, pr.up())
                    dve.wait_ge(s_t2, t2.next())
                    t = TT[:, 0:SEQ]
                    v.scalar_tensor_tensor(t, GB[:, 1:1 + SEQ], fpar(f, base + FR_W + 1), t, ALU.mult, ALU.add).then_inc(s_v, own.up())
                    if 0 in adds:
                        x_add(0, 1)
                    dve.wait_ge(s_v, own.at())
                    v.scalar_tensor_tensor(t, GB[:, 0:SEQ], fpar(f, base + FR_W), t, ALU.mult, ALU.add).then_inc(s_v, own.up())
                    if 1 in adds:
                        x_add(1, 0)
                    dve.wait_ge(s_v, own.at())
                    t = TT[:, SEQ:T]
                    st = fpar(f, base + FR_ST, 2 * NS).rearrange("p (b j) -> p j b", j=2)
                    v.scalar_tensor_tensor(t, st[:, 1, :], fpar(f, base + FR_W + 1), t, ALU.mult, ALU.add).then_inc(s_v, own.up())
                    dve.wait_ge(s_v, own.at())
                    v.scalar_tensor_tensor(t, st[:, 0, :], fpar(f, base + FR_W), t, ALU.mult, ALU.add).then_inc(s_gc, gc.up())

                def value(s, q):
                    dve.wait_ge(s_silu, silu.next())
                    dve.wait_ge(s_mm, mm.next())
                    if mh.due():
                        dve.wait_ge(s_mh, mh.at())
                    dve.wait_ge(s_v, own.at())
                    v.tensor_tensor(chunks(MM), side(s), chunks(TT), ALU.mult).then_inc(s_pr, pr.up())
                    dve.wait_ge(s_pr, pr.at())
                    v.tensor_tensor(MM, MM, RS, ALU.mult).then_inc(s_m, m_.up())
                    dve.wait_ge(s_mh, mh.next())
                    v.tensor_tensor(MID[:, q, 1, :], MM, MID[:, q, 0, :].bitcast(F32), ALU.subtract).then_inc(s_mid, mid.up())

                gate(0, 0)
                value(1, 0)
                gate(0, 1)
                value(1, 1)
                with turns(dve, 1, FT // 2, {mm: 12, pr: 12, t2: 2, own: 6, gc: 2, silu: 2, m_: 2, mh: 2, mid: 2}) as i:
                    gate(0, i * 2, adds=(0, 1))
                    for m in range(2, KT):
                        x_add(m, (m + 1) % 2)
                    value(1, 0)
                    gate(0, i * 2 + 1)
                    value(1, 1)
                residual(lambda o: 1 - o, None, True, R_MIX + 1 if l == 0 else None)
            ffn(0)

            heads = Count()
            norm_scale()
            for j in range(2):
                dve.wait_ge(s_mm, mm.next())
                v.tensor_tensor(chunks(WK[:, 4 + j, 0:T]), side(j), chunks(RS), ALU.mult).then_inc(s_pr, pr.up())
            dve.wait_ge(s_tab, 16)
            v.tensor_tensor(COS, COS, RS, ALU.mult).then_inc(s_v, own.up())
            dve.wait_ge(s_v, own.at())
            v.tensor_tensor(SIN, SIN, RS, ALU.mult).then_inc(s_v, own.up())
            dve.wait_ge(s_v, own.at())

            def raw_heads(s, t):
                dve.wait_ge(s_mm, mm.next())
                if heads.due():
                    dve.wait_ge(s_heads, heads.at())
                v.tensor_copy(chunks(WK[:, 1 + t % 2, 0:T]), side(s)).then_inc(s_pr, pr.up())

            def turn_heads(s, t):
                R = WK[:, 1 + t % 2, 0:T]
                T1 = WK[:, 3, 0:T]
                if heads.due():
                    dve.wait_ge(s_heads, heads.at())
                dve.wait_ge(s_pr, pr.at())
                v.tensor_tensor(T1, R, COS, ALU.mult).then_inc(s_v, own.up())
                dve.wait_ge(s_mm, mm.next())
                dve.wait_ge(s_v, own.at())
                v.tensor_tensor(chunks(R), side(s), chunks(SIN), ALU.mult).then_inc(s_pr, pr.up())
                dve.wait_ge(s_pr, pr.at())
                if t < 2:
                    v.tensor_tensor(WK[:, K_TILE[t], 0:T], T1, R, ALU.add).then_inc(s_heads, heads.up())
                    return
                q = t - 2
                j = q // 2
                rows = slice((j % 2) * HD, (j % 2 + 1) * HD)
                for o in range(2):
                    src = slice(o * HD, (o + 1) * HD)
                    v.tensor_tensor(QA[rows, j // 2, 2 * (q % 2) + o, :], T1[src, :], R[src, :], ALU.add).then_inc(s_heads, heads.up())

            raw_heads(0, 0)
            raw_heads(1, 1)
            for t in range(KT):
                turn_heads(0, t)
                if t == KT - 1:
                    turn_heads(0, KT)
                raw_heads(1, t)
            turn_heads(1, KT + 1)
            assert heads.n == HEADS

            attention_dve(dve)

            qt = QA[:, :, :, :].rearrange("p a g n -> p (a g) n")
            with turns(dve, 0, KT, {hh: 1, h: 1}) as m:
                split_lo(m, tile(qt, m))
            residual(lambda o: o, None, False, R_FFN + 1)
            ffn(1)

            token_scale()
            dve.wait_ge(s_rec, rec.at())
            dve.wait_ge(s_tr, tr.next())
            v.tensor_copy(WK[0:HIST + NS, 5, 0:D], PS[0:HIST + NS, 0:2, :].rearrange("p a n -> p (a n)")).then_inc(s_trr, trr.up())
            for l in range(2):
                dve.wait_ge(s_tr, tr.next(2))
                v.tensor_copy(GROWS[l][0:2 + NS, HALF_F:F], GATE_PS(1)).then_inc(s_trr, trr.up())
            for b in range(0, NB, 2):
                dve.wait_ge(s_tr, tr.next() if b == 0 else tr.next(2))
                v.tensor_scalar(YOUT[:, b, :], Y_PS(b), TOK[:, 2, b:b + 1], None, ALU.mult).then_inc(s_trr, trr.up())
            tr.n += 1
            dve.wait_ge(s_tr, tr.next())
            v.tensor_scalar(WK[0:NS, 4, 0:D], PS[0:NS, 0:2, :].rearrange("p a n -> p (a n)"),
                                    TOK[0:NS, 2, NB:NB + 1], None, ALU.mult).then_inc(s_trr, trr.up())

        @block.scalar
        def _(act):
            sc_ = nc.scalar
            act.dma_start(CST[:, :], a["const_small"]).then_inc(s_const, 16)
            r = lambda k, n=1: WK[k:k + n, 0, 0:D]
            rows = [(r(R_MIX, 2), a["norm_mix"]), (r(R_FFN, 2), a["norm_ffn"]),
                    (r(R_FIN), a["norm_final"].rearrange("(a n) -> a n", a=1)),
                    (r(R_B1, 2), a["conv_b_pw1"].rearrange("a (b n) -> (a b) n", b=2)),
                    (r(R_DW, CW), a["conv_w_dw"][0]), (r(R_BDW), a["conv_b_dw"]), (r(R_LNG), a["conv_ln_g"]),
                    (r(R_LNB), a["conv_ln_b"]), (r(R_B2), a["conv_b_pw2"]),
                    (WK[0:NS, 3, 0:D], a["x_sample"].rearrange("b s d -> (b s) d")),
                    (WK[0:1, 3, D:D + NH], a["attn_sinks"]), (SINKC[:, 0:1], a["attn_sinks"].rearrange("a h -> h a"))]
            hist = a["state_conv"].rearrange("a b k d -> (a b k) d")
            frow = WK[:, 4:7, :].rearrange("p a n -> p (a n)")
            half = NS * HIST // 2
            rows += [(WK[0:half, 1, 0:D], hist[0:half]), (WK[0:half, 2, 0:D], hist[half:2 * half])]
            fr = []
            for l in range(2):
                b = l * NFR
                fr += [(frow[b + FR_W:b + FR_B, 0:F], a["ffn_w_dw"][l]),
                       (frow[b + FR_B:b + FR_ST, 0:F], a["ffn_b_dw"][l:l + 1]),
                       (frow[b + FR_ST:b + NFR, 0:F], a["state_ffn"][l].rearrange("b k f -> (b k) f"))]
            assert len(rows) + len(fr) == ROW_DMAS
            for dst, src in rows + fr:
                act.dma_start(dst, src).then_inc(s_rows, 16)
            for b in range(NB):
                act.dma_start(XIN[:, b, :], a["x_prompt"][0, b * P:(b + 1) * P, :]).then_inc(s_x, 16)
            act.dma_start(a["new_conv_sample"][0, :, 0:HIST - 1, :], a["state_conv"][0, :, 1:HIST, :]).then_inc(s_st, 16)
            act.dma_start(a["new_ffn_sample"][:, :, 0, :], a["state_ffn"][:, :, 1, :]).then_inc(s_st, 16)
            for new, old in (("new_k_sample", "cache_k"), ("new_v_sample", "cache_v")):
                act.dma_start(a[new][0, :, 0:WIN - 1].rearrange("b w j d -> b (w j d)"),
                              a[old][0, :, 1:WIN].rearrange("b w j d -> b (w j d)")).then_inc(s_st, 16)

            own = Count()
            trr, pr, sq, acc = Count(), Count(), Count(), Count()
            hh, h, sums, root = Count(), Count(), Count(), Count()
            F_ = sc_.activation

            def square(src, dst, reader_back=1):
                act.wait_ge(s_acc, acc.at(reader_back))
                acc.n += 1
                F_(dst, src, ACT.Square).then_inc(s_sq, sq.up())

            def roots():
                act.wait_ge(s_sum, sums.next())
                F_(TOK[:, 1, 0:NB], PS[:, 6, 0:NB], ACT.Sqrt, scale=1.0 / D, bias=EPSC[:, :])
                F_(TOK[0:NS, 1, NB:NB + 1], PS[0:NS, 6, NB:NB + 1], ACT.Sqrt, scale=1.0 / D,
                   bias=EPSC[0:NS, :]).then_inc(s_root, root.up())

            def residual(row):
                acc.n += 1
                with turns(act, 0, KT // 2 - 1, {pr: 2, acc: 2, sq: 2}) as i:
                    for o in range(2):
                        act.wait_ge(s_pr, pr.next())
                        square(tile(X, i * 2 + o), SQ[o])
                act.wait_ge(s_pr, pr.next())
                square(X[:, KT - 2, :], SQ[0])
                if row is not None:
                    act.wait_ge(s_mm, pr.n + 1)
                    for m in range(2):
                        F_(H[:, 0, m, :], X[:, m, :], ACT.Identity, scale=par(m, row)).then_inc(s_hh, hh.up())
                act.wait_ge(s_pr, pr.next())
                square(X[:, KT - 1, :], SQ[1])
                if row is not None:
                    with turns(act, 2, KT, {hh: 1}) as m:
                        F_(htile(0, m), tile(X, m), ACT.Identity, scale=par(m, row)).then_inc(s_hh, hh.up())

            trr.n += 2
            acc.n += 2
            with turns(act, 0, KT, {trr: 1, hh: 1}) as m:
                act.wait_ge(s_trr, trr.next())
                F_(htile(0, m), tile(X, m), ACT.Identity, scale=par(m, R_MIX)).then_inc(s_hh, hh.up())
            with turns(act, 0, KT // 2, {acc: 2, sq: 2}) as i:
                for o in range(2):
                    square(tile(X, i * 2 + o), SQ[o])
            roots()
            sig, glu, tap0, gh, diag, td = (Count() for _ in range(6))

            def diagonals(i, D_, first):
                for k in range(D_.shape[2]):
                    F_(D_[:, 0, k, :], IDENT, ACT.Identity, scale=par(i, R_DW + CW - NT + first + k))
                    lo = TAPLO[:, bass.ds(i, 1), first + k:first + k + 1].rearrange("p a b -> p (a b)")
                    last = F_(D_[:, 1, k, :], IDENT, ACT.Identity, scale=lo)
                last.then_inc(s_diag, diag.up())
            GL, TG, SIG = (WK[:, k, :] for k in (4, 3, 5))
            act.sem_inc(s_sig, 1)
            act.sem_inc(s_tap0, 1)
            F_(TAPHI, PAR[:, :, R_DW + CW - NT:R_DW + CW], ACT.Copy).then_inc(s_taphi, 1)
            act.wait_ge(s_taplo, 1)
            diagonals(0, DIAGA, 0)

            def conv_act(i):
                act.wait_ge(s_pr, pr.next(2))
                F_(SIG[:, 0:T], TG[:, 0:T], ACT.Sigmoid, bias=par(i, R_B1 + 1)).then_inc(s_sig, sig.up())
                act.wait_ge(s_glu, glu.next())
                F_(GSPLIT[:, 0, 0:WKC], GL[:, 0:WKC], ACT.Copy).then_inc(s_gh, gh.up())
                F_(tile(CKEEP, i, 0, HIST + NS), GL[:, SEQ:WKC], ACT.Copy)
                F_(tile(CONV, i, 0, SEQ), GL[:, 0:SEQ], ACT.Identity, scale=par(i, R_DW), bias=par(i, R_BDW)).then_inc(s_tap0, tap0.up())
                diagonals(i, DIAGB, NTA)

            with turns(act, 0, KT - 1, {pr: 2, sig: 1, glu: 1, tap0: 1, gh: 1, diag: 2, td: 1}) as i:
                conv_act(i)
                act.wait_ge(s_td, td.next())
                diagonals(i + 1, DIAGA, 0)
            conv_act(KT - 1)
            acc.n += 1
            sums.n += 1
            cen, sqd = Count(), Count()
            for m in range(KT):
                act.wait_ge(s_conv, cen.next())
                if m >= 2:
                    act.wait_ge(s_sqd, sqd.next())
                F_(LNSQ[m % 2], tile(CONV, m), ACT.Square).then_inc(s_sq, sq.up())
            act.wait_ge(s_sqd, sqd.next(2))
            F_(chunks(RS), PS[:, 0:3, 0:CH], ACT.Sqrt, scale=1.0 / D, bias=EPSC[:, :]).then_inc(s_root, root.up())
            act.dma_start(WK[:, 7:9, 0:T], a["const_rope"].rearrange("p (a n) -> p a n", a=2)).then_inc(s_tab, 16)
            y = Count()
            h.n = KT
            for m in range(KT):
                if m < KT // 2:
                    act.wait_ge(s_conv, cen.next())
                else:
                    act.wait_ge(s_cg, m - KT // 2 + 1)
                if m >= 3:
                    act.wait_ge(s_h, h.next())
                F_(LNOUT[m % 3], CONV[:, m, :], ACT.Silu, scale=par(m, R_LNG), bias=par(m, R_LNB)).then_inc(s_silu, y.up())
                act.wait_ge(s_silu, y.at())
                F_(H[:, 0, m, :], LNOUT[m % 3], ACT.Copy).then_inc(s_hh, hh.up())
            h.n = 2 * KT
            residual(R_FFN)

            t2, gc, silu, m_, mh = (Count() for _ in range(5))
            silu.n = y.n
            GB, TT, MM = WK[:, 4, :], WK[:, 5, 0:T], WK[:, 6, 0:T]

            def ffn(l):
                roots()
                base = l * NFR

                def gate(f):
                    act.wait_ge(s_pr, pr.next())
                    F_(tile(GKEEP[:, l], f, 0, 2 + NS), GB[:, SEQ:2 + T], ACT.Copy)
                    F_(TT, GB[:, 2:2 + T], ACT.Identity, scale=fpar(f, base + FR_W + 2), bias=fpar(f, base + FR_B)).then_inc(s_t2, t2.up())
                    act.wait_ge(s_gc, gc.next())
                    F_(TT, TT, ACT.Silu).then_inc(s_silu, silu.up())

                def value(q):
                    pr.n += 1
                    act.wait_ge(s_m, m_.next())
                    F_(MID[:, q, 0, :], MM, ACT.Copy).then_inc(s_mh, mh.up())

                gate(0)
                value(0)
                gate(1)
                value(1)
                with turns(act, 1, FT // 2, {pr: 12, t2: 2, gc: 2, silu: 2, m_: 2, mh: 2}) as i:
                    gate(i * 2)
                    pr.n += KT
                    value(0)
                    gate(i * 2 + 1)
                    value(1)
                residual(R_MIX + 1 if l == 0 else None)
            ffn(0)

            roots()
            kvh = Count()
            act.wait_ge(s_mm, pr.n + 5 + 2 * KT)
            act.wait_ge(s_heads, 2)
            for p in range(2):
                F_(KR[:, 0, p, P:PADK], WK[:, K_TILE[p], 0:T], ACT.Copy).then_inc(s_kvh, kvh.up())
            F_(IDR[:, :], IDENT, ACT.Copy).then_inc(s_kvh, kvh.up())
            act.wait_ge(s_heads, HEADS)
            act.dma_start(WK[:, 7, 0:D], a["const_mask"]).then_inc(s_tab, 16)
            act.wait_ge(s_kvr, 1)
            F_(VR[:, 0, 1:NB + 1, :].rearrange("p (a b) n -> p a (b n)", b=2), PS[:, 0:4, :], ACT.Copy).then_inc(s_kvh, kvh.up())
            act.wait_ge(s_tab, 32)
            F_(MASK[:, :, :].rearrange("p a n -> p (a n)"), WK[:, 7, 0:D], ACT.Copy).then_inc(s_kvh, kvh.up())
            qh, sc, nm, ex = Count(), Count(), Count(), Count()
            pt, pth, pv, ov = Count(), Count(), Count(), Count()

            def q_hi(n, p):
                if n > 0:
                    act.wait_ge(s_sc, 4 * (n - 1) + 2 * p + 2)
                F_(QS[:, p, 0, :].rearrange("p (g n) -> p g n", g=GROUP), QA[:, p, :, n * P:(n + 1) * P], ACT.Copy).then_inc(s_qh, qh.up())

            def exps(n, p, hf):
                j = 2 * p + hf
                act.wait_ge(s_nm, nm.next(2))
                for g in range(GROUP):
                    F_(PX[:, hf, g, :], PS[:, 2 * hf + g // 2, (g % 2) * 256:(g % 2 + 1) * 256], ACT.Exp,
                       scale=SCALE, bias=SMALL[:, hf, 1, g:g + 1], accum_out=SMALL[:, hf, 3, g:g + 1])
                F_(SMALL[:, hf, 4, :], SMALL[:, hf, 2, :], ACT.Exp).then_inc(s_ex, ex.up())

            q_hi(0, 0)
            exps(*UNITS[0])
            q_hi(0, 1)
            exps(*UNITS[1])
            for u, (n, p, hf) in enumerate(UNITS):
                act.wait_ge(s_pt, pt.next())
                F_(PT[:, 0], PS[:, 4:6, :], ACT.Copy).then_inc(s_pth, pth.up())
                if u + 4 < len(UNITS) and UNITS[u + 4][2] == 0:
                    q_hi(*UNITS[u + 4][:2])
                if u + 2 < len(UNITS):
                    exps(*UNITS[u + 2])
                act.wait_ge(s_pv, pv.next())
                rows_ = slice(hf * HD, (hf + 1) * HD)
                F_(QA[rows_, p, :, n * P:(n + 1) * P],
                          PS[rows_, 6 + hf, :].rearrange("p (g n) -> p g n", g=GROUP), ACT.Copy).then_inc(s_ov, ov.up())
            sa = Count()
            act.wait_ge(s_svx, 1)
            ss = WK[0:NH, 7, 0:D + NS]
            F_(WK[0:NH, 6, 400:408], WK[0:NH, 6, 392:400], ACT.Exp, bias=SINKC[:, 0:1])
            F_(ss, ss, ACT.Exp).then_inc(s_sa, sa.up())
            act.wait_ge(s_sv, 5)
            qt = QA[:, :, :, :].rearrange("p a g n -> p (a g) n")
            with turns(act, 0, KT, {hh: 1}) as m:
                F_(htile(0, m), tile(qt, m), ACT.Copy).then_inc(s_hh, hh.up())
            pr.n += 12 + KT + 2
            residual(R_FFN + 1)
            ffn(1)

            xg = Count()
            act.wait_ge(s_acc, acc.at())
            for m in range(KT):
                F_(X[:, m, :], X[:, m, :], ACT.Identity, scale=par(m, R_FIN)).then_inc(s_xg, xg.up())
                if m == KT // 2:
                    roots()
            turned, taken = 1 + KT, 2 + KT
            ka = Count()
            for l in range(2):
                act.wait_ge(s_tr, turned + 2 + 2 * l)
                F_(GROWS[l][0:2 + NS, 0:HALF_F], GATE_PS(0), ACT.Copy).then_inc(s_ka, ka.up())
            act.wait_ge(s_rec, sums.n - 1)
            for b in range(1, NB, 2):
                act.wait_ge(s_tr, turned + 6 + b)
                F_(YOUT[:, b, :], Y_PS(b), ACT.Identity, scale=TOK[:, 2, b:b + 1]).then_inc(s_ya, 1)
            act.wait_ge(s_ka, ka.at())
            act.wait_ge(s_trr, taken + 3)
            act.dma_start(a["new_conv_prompt"][0, 0], WK[0:HIST, 5, 0:D]).then_inc(s_st, 16)
            act.dma_start(a["new_conv_sample"][0, :, HIST - 1, :], WK[HIST:HIST + NS, 5, 0:D]).then_inc(s_st, 16)
            for l in range(2):
                act.dma_start(a["new_ffn_prompt"][l, 0], GROWS[l][0:2, 0:F]).then_inc(s_st, 16)
                act.dma_start(a["new_ffn_sample"][l, :, 1, :], GROWS[l][2:2 + NS, 0:F]).then_inc(s_st, 16)

        def attention_pe(pe, transpose, PASSES, pr):
            matmul = nc.tensor.matmul
            kv, qs, sc, ex = Count(), Count(), Count(), Count()
            pn, pt, ptl, pth = Count(), Count(), Count(), Count()
            pv, ov = Count(), Count()
            smm, sdv = Count(), Count()
            pe.wait_ge(s_pr, pr.at(1))
            for b in range(NB):
                if b == 2 * NCH:
                    pe.wait_ge(s_pr, pr.at())
                for j in range(2):
                    transpose(PS[:, b // 2, (b % 2) * 256 + j * P:(b % 2) * 256 + (j + 1) * P],
                              WK[:, 4 + j, b * P:(b + 1) * P])
            for j in range(2):
                transpose(PS[0:NS, 4, j * P:(j + 1) * P], WK[:, 4 + j, SEQ:T])
                kt = WK[:, K_TILE[j], :]
                transpose(PS[:, 5, j * P:(j + 1) * P], kt[:, SEQ - P:SEQ])
                last = transpose(PS[0:NS, 4, (2 + j) * P:(3 + j) * P], kt[:, SEQ:T])
            last.then_inc(s_kvo, 1)
            pe.wait_ge(s_kv, kv.next(KV_READY))
            pe.wait_ge(s_kvh, 5)

            def scores(n, p, hf):
                if hf == 0:
                    pe.wait_ge(s_qs, qs.next())
                if ex.due(1):
                    pe.wait_ge(s_ex, ex.at(1))
                ex.n += 1
                rows = slice(hf * HD, (hf + 1) * HD)
                first = 0 if n == 0 else 1
                for b in range(2):
                    for g in (2 * b, 2 * b + 1):
                        for q, (kp, qp) in enumerate(PASSES):
                            out = PS[:, 2 * hf + b, (g % 2) * 256:(g % 2 + 1) * 256]
                            matmul(out, QS[rows, p, qp, g * P:(g + 1) * P],
                                   KR[rows, kp, p, n * P:n * P + 2 * P],
                                   start=(g % 2 == 0 and q == 0), stop=False, skip_group_check=True)
                    last = matmul(PS[:, 2 * hf + b, :], IDR[:, :], MASK[:, first, :], start=False, stop=True,
                                  skip_group_check=True)
                last.then_inc(s_sc, sc.up())

            def turn(n, p, hf):
                pe.wait_ge(s_pn, pn.next())
                if ptl.due():
                    pe.wait_ge(s_ptl, ptl.at())
                ptl.n += 1
                for s in range(2):
                    for g in range(GROUP):
                        last = transpose(PS[:, 4 + s, g * P:(g + 1) * P], PX[:, hf, g, s * P:(s + 1) * P])
                last.then_inc(s_pt, pt.up())

            def heads(n, p, hf):
                if ov.due(1):
                    pe.wait_ge(s_ov, ov.at(1))
                ov.n += 1
                pth.n += 1
                pe.wait_ge(s_pth, pth.at())
                for q, (vp, pp) in enumerate(((0, 0), (1, 0), (0, 1))):
                    if pp == 1:
                        pe.wait_ge(s_ptl, ptl.at())
                    for s in range(2):
                        vb = VR[:, :, n + s, p * P:(p + 1) * P]
                        last = matmul(PS[:, 6 + hf, :], vb[:, vp, :], PT[:, pp, s, :],
                                      start=(s == 0 and q == 0), stop=(s == 1 and q == 2))
                last.then_inc(s_pv, pv.up())

            for u in range(3):
                scores(*UNITS[u])
            for u in range(len(UNITS)):
                turn(*UNITS[u])
                if u + 3 < len(UNITS):
                    scores(*UNITS[u + 3])
                if u + 1 == len(UNITS):
                    pe.wait_ge(s_ex, ex.at())
                    pe.wait_ge(s_cache, 32)
                    for p in range(2):
                        for k in range(NS):
                            last = transpose(PS[:, 2 * p + k // 4, (k % 4) * P:(k % 4 + 1) * P],
                                             WK[:, 0:2, 0:D][:, k // 4, (k % 4) * 256 + p * P:(k % 4) * 256 + (p + 1) * P])
                    last.then_inc(s_sm, smm.up())
                heads(*UNITS[u])

            pe.wait_ge(s_ov, ov.at())
            pe.wait_ge(s_sv, sdv.next(2))
            kct = WK[:, 4:6, 0:D].rearrange("p a (w r) -> p a w r", w=8)
            for b in range(NS):
                for p in range(2):
                    qb = WK[:, 6, 0:256].rearrange("p (a b h) -> p a b h", a=2, b=NS)[:, p, b, :]
                    matmul(PS[0:NH, 4 + b // 4, (b % 4) * P:(b % 4 + 1) * P], qb,
                           kct[:, p, :, b * 16:(b + 1) * 16], start=(p == 0), stop=(p == 1))
            for b in range(NS):
                for p in range(2):
                    qb = WK[:, 6, 0:256].rearrange("p (a b h) -> p a b h", a=2, b=NS)[:, p, b, :]
                    last = matmul(PS[0:NH, 6, b:b + 1], qb, WK[:, K_TILE[p], SEQ + b:SEQ + b + 1], start=(p == 0), stop=(p == 1))
            last.then_inc(s_sm, smm.up())
            pe.wait_ge(s_sv, sdv.next())
            for k in range(8):
                transpose(PS[:, 0, k * NH:(k + 1) * NH], WK[0:NH, 7, k * P:(k + 1) * P])
            last = transpose(PS[0:NS, 0, P:P + NH], WK[0:NH, 7, D:D + NS])
            last.then_inc(s_sm, smm.up())
            pe.wait_ge(s_sv, sdv.next())
            pnb = WK[0:NS, 6, 256:256 + P]
            for p in range(2):
                for k in range(8):
                    matmul(PS[:, 1, p * P:(p + 1) * P], WK[:, 2 + k // 4, (k % 4) * 256 + p * P:(k % 4) * 256 + (p + 1) * P],
                           PBLK[:, k, :, :].rearrange("p b h -> p (b h)"), start=(k == 0), stop=False)
                last = matmul(PS[:, 1, p * P:(p + 1) * P], WK[0:NS, 8, p * P:(p + 1) * P], pnb, start=False, stop=True)
            last.then_inc(s_sm, smm.up())
            pe.wait_ge(s_sv, sdv.next())

        @block.tensor
        def _(pe):
            tr, trr = Count(), Count()
            mm, pr = Count(), Count()
            w, started = Count(), Count()
            h = Count()
            acc = Count()
            sums, rec, bc, bcr = (Count() for _ in range(4))
            mid = Count()
            matmul = nc.tensor.matmul
            PASSES = ((0, 0), (0, 1), (1, 0))

            def begin_group():
                if pr.due(1):
                    pe.wait_ge(s_pr, pr.at(1))
                pr.n += 1

            def dense(side, slot, wait_h=False, hooks={}):
                pe.wait_ge(s_w, w.next())
                begin_group()
                for k in range(KT):
                    if wait_h:
                        pe.wait_ge(s_h, h.next())
                    for q, (wp, hp) in enumerate(PASSES):
                        for c in range(NCH):
                            last = matmul(PS[:, 3 * side + c, 0:CH], W[:, slot, wp, k * P:(k + 1) * P],
                                          H[:, hp, k, c * CH:(c + 1) * CH],
                                          start=(k == 0 and q == 0), stop=(k == KT - 1 and q == 2))
                            if k == 0 and q == 0 and c == 0:
                                last.then_inc(s_wstart, started.up())
                    if k in hooks:
                        hooks[k]()
                last.then_inc(s_mm, mm.up())

            def down(slot):
                pe.wait_ge(s_w, w.next())
                for m in range(4):
                    begin_group()
                    side = (m + 1) % 2
                    for t in range(2):
                        for q, (wp, hp) in enumerate(PASSES):
                            for c in range(NCH):
                                last = matmul(PS[:, 3 * side + c, 0:CH],
                                              W[:, slot, wp, t * BANK + m * P:t * BANK + (m + 1) * P],
                                              MID[:, t, hp, c * CH:(c + 1) * CH],
                                              start=(t == 0 and q == 0), stop=(t == 1 and q == 2))
                                if m == 0 and t == 0 and q == 0 and c == 0:
                                    last.then_inc(s_wstart, started.up())
                    last.then_inc(s_mm, mm.up())

            def token_sums():
                acc.n = next(ACCS)
                pe.wait_ge(s_acc, acc.at())
                for b in range(NB + 1):
                    n = P if b < NB else NS
                    last = matmul(PS[0:n, 6, b:b + 1], ACC[:, b * P:b * P + n], ONES[:, 0:1], start=True, stop=True)
                last.then_inc(s_sum, sums.up())

            def broadcast():
                pe.wait_ge(s_rec, rec.next())
                for b in range(NB):
                    last = matmul(PS[:, 6 + b // 4, (b % 4) * P:(b % 4 + 1) * P],
                                  TOK[:, 2, b:b + 1].broadcast_to((P, P)), IDENT, start=True, stop=True)
                last.then_inc(s_bc, bc.up())

            def broadcast_samples():
                pe.wait_ge(s_bcr, bcr.next())
                matmul(PS[:, 6, 0:NS], TOK[0:NS, 2, NB:NB + 1].broadcast_to((NS, P)), IDENT[0:NS, 0:NS],
                       start=True, stop=True).then_inc(s_bc, bc.up())
                bcr.n += 1

            def transpose(out, in_):
                n = in_.shape[0]
                return nc.tensor.transpose(out, in_, IDENT[0:n, 0:n])

            pe.wait_ge(s_const, 16)
            pe.wait_ge(s_rows, 16 * ROW_DMAS)
            for m in range(KT):
                last = transpose(PS[:, 0, m * NPAR:(m + 1) * NPAR], WK[0:NPAR, 0, m * P:(m + 1) * P])
                for hf in range(2):
                    rows = HIST * NS // 2
                    last = transpose(PS[:, 1 + m // 2, (m % 2) * 240 + hf * rows:(m % 2) * 240 + (hf + 1) * rows],
                                     WK[0:rows, 1 + hf, m * P:(m + 1) * P])
            for f in range(FT):
                rows = WK[0:2 * NFR, 4:7, :].rearrange("p a n -> p (a n)")
                last = transpose(PS[:, 5 + f // 12, (f % 12) * 2 * NFR:(f % 12 + 1) * 2 * NFR], rows[:, f * P:(f + 1) * P])
            for m in range(KT):
                last = transpose(PS[:, 7, m * NS:(m + 1) * NS], WK[0:NS, 3, m * P:(m + 1) * P])
            last = matmul(PS[:, 7, 64:64 + NH], ONES[0:1, :], WK[0:1, 3, D:D + NH], start=True, stop=True)
            last.then_inc(s_tr, tr.up())
            pe.wait_ge(s_trr, trr.next(2))
            pe.wait_ge(s_x, 16 * NB)
            for m in range(KT):
                o = m % 2
                pe.wait_ge(s_trr, trr.at(1))
                trr.n += 1
                for b in range(NB):
                    last = transpose(PS[:, 2 * o + b // 4, (b % 4) * P:(b % 4 + 1) * P], XIN[:, b, m * P:(m + 1) * P])
                last.then_inc(s_tr, tr.up())
            pe.wait_ge(s_trr, trr.at())

            ACCS = iter(acc_marks)
            dense(0, 0, wait_h=True)
            token_sums()
            dense(1, 1, hooks={2: broadcast, 5: broadcast_samples})
            gs, diag, td, tt = (Count() for _ in range(4))

            def last_taps():
                pe.wait_ge(s_diag, diag.next())
                pe.wait_ge(s_gs, gs.next())
                if tt.due():
                    pe.wait_ge(s_tt, tt.at())
                tt.n += 1
                for k in range(NT):
                    if k == NTA:
                        pe.wait_ge(s_diag, diag.next())
                    diagonal = DIAGA[:, :, k, :] if k < NTA else DIAGB[:, :, k - NTA, :]
                    for q, (wp, gp) in enumerate(PASSES):
                        for c in range(2):
                            col = CW - NT + k + c * BANK
                            last = matmul(PS[:, 6 + c, :], diagonal[:, wp, :], GSPLIT[:, gp, col:col + BANK],
                                          start=(k == 0 and q == 0), stop=(k == NT - 1 and q == 2))
                last.then_inc(s_td, td.up())
            dense(0, 0)
            last_taps()
            dense(1, 1)
            with turns(pe, 2, KT, {w: 2, started: 2, mm: 2, pr: 2, gs: 1, diag: 2, td: 1, tt: 1}):
                dense(0, 0)
                last_taps()
                dense(1, 1)
            last_taps()
            pe.wait_ge(s_cs, KT)
            for c in range(NCH):
                last = matmul(PS[:, c, 0:CH], ONES, ACC[:, c * CH:(c + 1) * CH], start=True, stop=True)
            last.then_inc(s_sum, sums.up())
            sq, sqd = Count(), Count()
            sq.n = KT
            for m in range(KT):
                pe.wait_ge(s_sq, sq.next())
                for c in range(NCH):
                    last = matmul(PS[:, c, 0:CH], ONES, LNSQ[m % 2][:, c * CH:(c + 1) * CH],
                                  start=(m == 0), stop=(m == KT - 1))
                last.then_inc(s_sqd, sqd.up())
            dense(0, 0, wait_h=True)
            dense(1, 1)
            with turns(pe, 1, KT // 2, {w: 2, started: 2, mm: 2, pr: 2}):
                dense(0, 0)
                dense(1, 1)

            def ffn():
                dense(0, 0, wait_h=True, hooks={2: token_sums})
                dense(1, 1, hooks={1: broadcast, 4: broadcast_samples})
                dense(0, 0)
                dense(1, 1)
                with turns(pe, 1, FT // 2, {w: 6, started: 6, mm: 12, pr: 12, mid: 2}):
                    dense(0, 0)
                    pe.wait_ge(s_mid, mid.next(2))
                    down(1)
                    down(0)
                    dense(1, 1)
                    dense(0, 0)
                    dense(1, 1)
                pe.wait_ge(s_mid, mid.next(2))
                down(0)
                down(1)
            ffn()

            def swap(side, t):
                begin_group()
                raw_group = t + 2 if t < 2 else 2 * t + 1 + (t > KT)
                pe.wait_ge(s_pr, before + raw_group + 1)
                for c in range(NCH):
                    last = matmul(PS[:, 3 * side + c, 0:CH], PERM, WK[:, 1 + t % 2, c * CH:(c + 1) * CH],
                                  start=True, stop=True)
                last.then_inc(s_mm, mm.up())
            before = pr.n
            dense(0, 0, wait_h=True, hooks={2: token_sums})
            dense(1, 1, hooks={1: broadcast, 4: broadcast_samples})
            dense(0, 0)
            dense(1, 1)
            for t in range(KT):
                swap(0, t)
                if t < KT - 1:
                    dense(1, t % 2)
                else:
                    dense(1, t % 2, hooks={1: lambda: swap(0, KT)})
            swap(1, KT + 1)

            attention_pe(pe, transpose, PASSES, pr)

            dense(0, 0, wait_h=True)
            dense(1, 1)
            with turns(pe, 1, KT // 2, {w: 2, started: 2, mm: 2, pr: 2}):
                dense(0, 0)
                dense(1, 1)
            ffn()

            token_sums()
            pe.wait_ge(s_pr, pr.at())
            for m in range(KT):
                last = transpose(PS[0:HIST + NS, m // 4, (m % 4) * P:(m % 4 + 1) * P], CKEEP[:, m, :])
            last.then_inc(s_tr, tr.up())
            trr.n += 1
            for l in range(2):
                for part in range(2):
                    if l == 1 and part == 0:
                        pe.wait_ge(s_ka, 1)
                    if l == 1 and part == 1:
                        pe.wait_ge(s_trr, trr.next())
                    if l == 0 and part == 1:
                        pe.wait_ge(s_root, sums.n)
                    for f in range(FT // 2):
                        last = transpose(GATE_PS(part)[:, f * P:(f + 1) * P], GKEEP[:, l, part * FT // 2 + f, :])
                    last.then_inc(s_tr, tr.up())
            trr.n += 1
            pe.wait_ge(s_xg, KT)
            pe.wait_ge(s_ka, 2)
            pe.wait_ge(s_trr, trr.at())
            for b in range(NB):
                if b >= 4 and b % 2 == 0:
                    pe.wait_ge(s_trr, trr.next())
                elif b >= 4:
                    pe.wait_ge(s_ya, b // 2 - 1)
                for m in range(KT):
                    last = transpose(Y_PS(b)[:, m * P:(m + 1) * P], X[:, m, b * P:(b + 1) * P])
                last.then_inc(s_tr, tr.up())
            pe.wait_ge(s_trr, trr.next())
            for m in range(KT):
                last = transpose(PS[0:NS, m // 4, (m % 4) * P:(m % 4 + 1) * P], X[:, m, SEQ:T])
            last.then_inc(s_tr, tr.up())


_INS = ["x_prompt", "x_sample", "state_conv", "cache_k", "cache_v", "state_ffn", "norm_mix", "norm_ffn", "norm_final",
        "conv_w_pw1", "conv_b_pw1", "conv_w_dw", "conv_b_dw", "conv_ln_g", "conv_ln_b", "conv_w_pw2", "conv_b_pw2",
        "attn_w_qkv", "attn_sinks", "attn_w_o", "ffn_w_in", "ffn_w_dw", "ffn_b_dw", "ffn_w_down"]
_OUTS = [("y_prompt", (1, SEQ, D)), ("y_sample", (NS, 1, D)),
         ("new_conv_prompt", (1, 1, HIST, D)), ("new_conv_sample", (1, NS, HIST, D)),
         ("new_k_prompt", (1, 1, WIN, NKV, HD)), ("new_v_prompt", (1, 1, WIN, NKV, HD)),
         ("new_k_sample", (1, NS, WIN, NKV, HD)), ("new_v_sample", (1, NS, WIN, NKV, HD)),
         ("new_ffn_prompt", (2, 1, 2, F)), ("new_ffn_sample", (2, NS, 2, F))]


def kernel(**inputs):
    import concourse.bacc as bacc
    from concourse.bass_utils import run_bass_kernel_spmd

    nc = bacc.Bacc("TRN2", target_bir_lowering=False, num_devices=1)
    arrays = {n: np.ascontiguousarray(inputs[n]) for n in _INS}
    arrays["const_small"], arrays["const_mask"], arrays["const_rope"] = constants()
    aps = {}
    for name, x in arrays.items():
        aps[name] = nc.dram_tensor(f"in_{name}", x.shape, F32, kind="ExternalInput").ap()
    for name, shape in _OUTS:
        aps[name] = nc.dram_tensor(f"out_{name}", shape, F32, kind="ExternalOutput").ap()
    build(nc, aps)
    r = run_bass_kernel_spmd(nc, [{f"in_{n}": x for n, x in arrays.items()}], core_ids=[0])
    return tuple(r.results[0][f"out_{name}"] for name, _ in _OUTS)
```
